# Optimizing a Trainium2 kernel written in Bass

```python
import math
import jax, jax.numpy as jnp
from jax import lax
import numpy as np
import jax
import jax.numpy as jnp

D_MODEL = 1024
BATCH = 1
SEQ = 512
DEPTH = 2

EPS = 1e-6
HEAD_DIM = 64
Q_BLOCK = 128
LRU_WIDTH = 512
LRU_BLOCKS = 8
LRU_BLOCK = LRU_WIDTH // LRU_BLOCKS
CONV_WIDTH = 4
LRU_C = 8.0
NSA_HEADS = 8
NSA_KV_GROUPS = 2
NSA_HPG = NSA_HEADS // NSA_KV_GROUPS
CMP_LEN = 32
CMP_STRIDE = 16
CMP_HIDDEN = 128
SLC_LEN = 64
SLC_TOPN = 8
WIN = 512
FORCE_SCORE = 1e4
DSA_HEADS = 16
DSA_KV_HEADS = 2
DSA_HPG = DSA_HEADS // DSA_KV_HEADS
IDX_HEADS = 8
IDX_DIM = 64
IDX_TOPK_MAX = 256
D_FF = -(-8 * D_MODEL // (3 * 256)) * 256
NSA_Q = NSA_HEADS * HEAD_DIM
NSA_KV = NSA_KV_GROUPS * HEAD_DIM
IN0_SIZES = (LRU_WIDTH, LRU_WIDTH, NSA_Q, NSA_KV, NSA_KV, NSA_KV, NSA_KV, NSA_KV, NSA_KV, NSA_HEADS * 3)
IN0 = sum(IN0_SIZES)
MIX0 = LRU_WIDTH + NSA_Q
IN1_SIZES = (DSA_HEADS * HEAD_DIM, DSA_KV_HEADS * HEAD_DIM, DSA_KV_HEADS * HEAD_DIM, IDX_HEADS * IDX_DIM, IDX_DIM, IDX_HEADS)
IN1 = sum(IN1_SIZES)
MIX1 = DSA_HEADS * HEAD_DIM


def _split(t, sizes):
    return jnp.split(t, np.cumsum(sizes)[:-1].tolist(), axis=-1)

def rmsnorm(x, g):
    xf = x.astype(jnp.float32)
    y = xf * lax.rsqrt(jnp.mean(xf * xf, axis=-1, keepdims=True) + EPS)
    return (y * g.astype(jnp.float32)).astype(x.dtype)

def modulate(x, g, shift, scale):
    return rmsnorm(x, g) * (1.0 + scale[:, None, :]) + shift[:, None, :]

def masked_softmax(s, mask):
    s = jnp.where(mask, s.astype(jnp.float32), -jnp.inf)
    m = jnp.max(s, axis=-1, keepdims=True)
    m = jnp.where(jnp.isfinite(m), m, 0.0)
    p = jnp.exp(s - m)
    return p / jnp.maximum(jnp.sum(p, axis=-1, keepdims=True), 1e-30)

def swiglu(h, wg, wu, wd):
    return (jax.nn.silu(h @ wg) * (h @ wu)) @ wd

def adaln(c, w_mod, b_mod):
    mod = jax.nn.silu(c) @ w_mod + b_mod
    return jnp.split(mod, 6, axis=-1)

def causal_conv(x, w, b):
    S = x.shape[1]
    xp = jnp.pad(x, ((0, 0), (CONV_WIDTH - 1, 0), (0, 0)))
    out = xp[:, 0:S] * w[0]
    for k in range(1, CONV_WIDTH):
        out = out + xp[:, k:k + S] * w[k]
    return out + b

def rg_lru(x, wa, ba, wx, bx, lam):
    B, S, _ = x.shape
    xf = x.astype(jnp.float32)
    xb = xf.reshape(B, S, LRU_BLOCKS, LRU_BLOCK)
    r = jax.nn.sigmoid(jnp.einsum('bshi,hij->bshj', xb, wa).reshape(B, S, LRU_WIDTH) + ba)
    i = jax.nn.sigmoid(jnp.einsum('bshi,hij->bshj', xb, wx).reshape(B, S, LRU_WIDTH) + bx)
    log_a = -LRU_C * r * jax.nn.softplus(-lam.astype(jnp.float32))
    a = jnp.exp(log_a)
    mult = jnp.sqrt(-jnp.expm1(2.0 * log_a))
    mult = jnp.where((jnp.arange(S) == 0)[None, :, None], 1.0, mult)
    u = mult * (i * xf)

    def combine(e1, e2):
        a1, b1 = e1
        a2, b2 = e2
        return a1 * a2, a2 * b1 + b2

    _, h = lax.associative_scan(combine, (a, u), axis=1)
    return h.astype(x.dtype)

def compress_blocks(kv, pe, w1, w2):
    B, S, G, D = kv.shape
    nc = (S - CMP_LEN) // CMP_STRIDE + 1
    idx = jnp.arange(nc)[:, None] * CMP_STRIDE + jnp.arange(CMP_LEN)[None, :]
    blk = kv[:, idx] + pe[:, None, :]
    flat = blk.transpose(0, 1, 3, 2, 4).reshape(B, nc, G, CMP_LEN * D)
    return jax.nn.gelu(flat @ w1) @ w2

def nsa_mixer(q, k_cmp, v_cmp, k_slc, v_slc, k_win, v_win, gates, pe_k, w1_k, w2_k, pe_v, w1_v, w2_v):
    B, S = q.shape[:2]
    G, R, D = NSA_KV_GROUPS, NSA_HPG, HEAD_DIM
    scale = D ** -0.5
    nc = (S - CMP_LEN) // CMP_STRIDE + 1
    nsel = S // SLC_LEN
    n_top = min(SLC_TOPN, nsel)
    rs = lambda t: t.reshape(B, S, G, D)
    kc = compress_blocks(rs(k_cmp), pe_k, w1_k, w2_k)
    vc = compress_blocks(rs(v_cmp), pe_v, w1_v, w2_v)
    ks = rs(k_slc).reshape(B, nsel, SLC_LEN, G, D).transpose(0, 3, 1, 2, 4)
    vs = rs(v_slc).reshape(B, nsel, SLC_LEN, G, D).transpose(0, 3, 1, 2, 4)
    pad = ((0, 0), (WIN, 0), (0, 0), (0, 0))
    kw_pad = jnp.pad(rs(k_win), pad)
    vw_pad = jnp.pad(rs(v_win), pad)
    c_start = jnp.arange(nc) * CMP_STRIDE
    c_end = c_start + CMP_LEN - 1
    j_start = jnp.arange(nsel) * SLC_LEN
    overlap = ((c_start[:, None] < j_start[None, :] + SLC_LEN)
               & (c_start[:, None] + CMP_LEN > j_start[None, :])).astype(jnp.float32)
    jj = jnp.arange(nsel)
    b_i = jnp.arange(B)[:, None, None, None]
    g_i = jnp.arange(G)[None, :, None, None]

    def block(ib):
        t0 = ib * Q_BLOCK
        tq = t0 + jnp.arange(Q_BLOCK)
        qc = lax.dynamic_slice_in_dim(q, t0, Q_BLOCK, axis=1).reshape(B, Q_BLOCK, G, R, D)
        gc = lax.dynamic_slice_in_dim(gates, t0, Q_BLOCK, axis=1).reshape(B, Q_BLOCK, G, R, 3)
        s = jnp.einsum('bqgrd,bcgd->bgrqc', qc, kc) * scale
        p_cmp = masked_softmax(s, c_end[None, :] <= tq[:, None])
        o_cmp = jnp.einsum('bgrqc,bcgd->bqgrd', p_cmp, vc)
        imp = jnp.einsum('bgrqc,cj->bgqj', p_cmp, overlap)
        cur = tq // SLC_LEN
        forced = (jj[None, :] == 0) | (jj[None, :] == cur[:, None]) | (jj[None, :] == cur[:, None] - 1)
        imp = jnp.where(forced, FORCE_SCORE, imp)
        imp = jnp.where(jj[None, :] <= cur[:, None], imp, -jnp.inf)
        _, sel = lax.top_k(imp, n_top)
        kg = ks[b_i, g_i, sel].reshape(B, G, Q_BLOCK, n_top * SLC_LEN, D)
        vg = vs[b_i, g_i, sel].reshape(B, G, Q_BLOCK, n_top * SLC_LEN, D)
        kpos = sel[..., None] * SLC_LEN + jnp.arange(SLC_LEN)
        smask = (kpos <= tq[:, None, None]).reshape(B, G, 1, Q_BLOCK, n_top * SLC_LEN)
        s = jnp.einsum('bqgrd,bgqkd->bgrqk', qc, kg) * scale
        o_slc = jnp.einsum('bgrqk,bgqkd->bqgrd', masked_softmax(s, smask), vg)
        kw = lax.dynamic_slice_in_dim(kw_pad, t0, WIN + Q_BLOCK, axis=1)
        vw = lax.dynamic_slice_in_dim(vw_pad, t0, WIN + Q_BLOCK, axis=1)
        kpw = t0 - WIN + jnp.arange(WIN + Q_BLOCK)
        wmask = (kpw[None, :] >= 0) & (kpw[None, :] <= tq[:, None]) & (kpw[None, :] > tq[:, None] - WIN)
        s = jnp.einsum('bqgrd,bkgd->bgrqk', qc, kw) * scale
        o_win = jnp.einsum('bgrqk,bkgd->bqgrd', masked_softmax(s, wmask), vw)
        o = gc[..., 0:1] * o_cmp + gc[..., 1:2] * o_slc + gc[..., 2:3] * o_win
        return o.reshape(B, Q_BLOCK, G * R * D).astype(q.dtype)

    out = lax.map(block, jnp.arange(S // Q_BLOCK))
    return out.transpose(1, 0, 2, 3).reshape(B, S, G * R * D)

def dsa_mixer(q, k, v, q_idx, k_idx, w_idx):
    B, S = q.shape[:2]
    G, R, D = DSA_KV_HEADS, DSA_HPG, HEAD_DIM
    scale = D ** -0.5
    n_keep = min(IDX_TOPK_MAX, S // 4)
    kk = k.reshape(B, S, G, D)
    vv = v.reshape(B, S, G, D)
    qi_all = q_idx.reshape(B, S, IDX_HEADS, IDX_DIM)
    kpos = jnp.arange(S)
    b_i = jnp.arange(B)[:, None, None]

    def block(ib):
        t0 = ib * Q_BLOCK
        tq = t0 + jnp.arange(Q_BLOCK)
        qi = lax.dynamic_slice_in_dim(qi_all, t0, Q_BLOCK, axis=1)
        wi = lax.dynamic_slice_in_dim(w_idx, t0, Q_BLOCK, axis=1)
        sc = jax.nn.relu(jnp.einsum('bqhd,bsd->bqhs', qi, k_idx) * IDX_DIM ** -0.5)
        idx_score = jnp.einsum('bqhs,bqh->bqs', sc.astype(jnp.float32), wi.astype(jnp.float32)) * IDX_HEADS ** -0.5
        idx_score = jnp.where(kpos[None, :] <= tq[:, None], idx_score, -jnp.inf)
        _, sel = lax.top_k(idx_score, n_keep)
        kg = kk[b_i, sel]
        vg = vv[b_i, sel]
        qc = lax.dynamic_slice_in_dim(q, t0, Q_BLOCK, axis=1).reshape(B, Q_BLOCK, G, R, D)
        s = jnp.einsum('bqgrd,bqkgd->bgrqk', qc, kg) * scale
        mask = (sel <= tq[None, :, None])[:, None, None]
        o = jnp.einsum('bgrqk,bqkgd->bqgrd', masked_softmax(s, mask), vg)
        return o.reshape(B, Q_BLOCK, G * R * D).astype(q.dtype)

    out = lax.map(block, jnp.arange(S // Q_BLOCK))
    return out.transpose(1, 0, 2, 3).reshape(B, S, G * R * D)

def layer_ab(x, c, norm_mix, norm_ffn, mod_w, mod_b, w_in, conv_w, conv_b, wa, ba, wx, bx, lam,
             pe_k, w1_k, w2_k, pe_v, w1_v, w2_v, w_out, wg, wu, wd):
    sh_m, sc_m, g_m, sh_f, sc_f, g_f = adaln(c, mod_w, mod_b)
    h = modulate(x, norm_mix, sh_m, sc_m)
    (a_gate, a_x, q, kc, vc, ks, vs, kw, vw, gts) = _split(h @ w_in, IN0_SIZES)
    y_a = rg_lru(causal_conv(a_x, conv_w, conv_b), wa, ba, wx, bx, lam) * jax.nn.gelu(a_gate)
    y_b = nsa_mixer(q, kc, vc, ks, vs, kw, vw, jax.nn.sigmoid(gts), pe_k, w1_k, w2_k, pe_v, w1_v, w2_v)
    x = x + g_m[:, None, :] * (jnp.concatenate([y_a, y_b], axis=-1) @ w_out)
    h = modulate(x, norm_ffn, sh_f, sc_f)
    return x + g_f[:, None, :] * swiglu(h, wg, wu, wd)

def layer_c(x, c, norm_mix, norm_ffn, mod_w, mod_b, w_in, w_out, wg, wu, wd):
    sh_m, sc_m, g_m, sh_f, sc_f, g_f = adaln(c, mod_w, mod_b)
    h = modulate(x, norm_mix, sh_m, sc_m)
    q, k, v, q_idx, k_idx, w_idx = _split(h @ w_in, IN1_SIZES)
    x = x + g_m[:, None, :] * (dsa_mixer(q, k, v, q_idx, k_idx, w_idx) @ w_out)
    h = modulate(x, norm_ffn, sh_f, sc_f)
    return x + g_f[:, None, :] * swiglu(h, wg, wu, wd)

def first_inputs(seed: int = 0) -> dict:
    key = jax.random.key(seed)
    keys = iter(jax.random.split(key, 64))

    def nrm(shape, s):
        return jax.random.normal(next(keys), shape, jnp.float32) * s

    def gain(n):
        return 1.0 + nrm((n,), 0.05)

    D = D_MODEL
    a0 = jax.random.uniform(next(keys), (LRU_WIDTH,), jnp.float32, minval=0.9, maxval=0.999)
    r0 = a0 ** (1.0 / LRU_C)
    lam = jnp.log(r0) - jnp.log1p(-r0)
    return {
        "x": nrm((BATCH, SEQ, D), 1.0),
        "c": nrm((BATCH, D), 1.0),
        "l0_norm_mix": gain(D),
        "l0_norm_ffn": gain(D),
        "l0_mod_w": nrm((D, 6 * D), 0.5 * D ** -0.5),
        "l0_mod_b": nrm((6 * D,), 0.01),
        "l0_w_in": nrm((D, IN0), D ** -0.5),
        "l0_conv_w": nrm((CONV_WIDTH, LRU_WIDTH), CONV_WIDTH ** -0.5),
        "l0_conv_b": nrm((LRU_WIDTH,), 0.01),
        "l0_lru_wa": nrm((LRU_BLOCKS, LRU_BLOCK, LRU_BLOCK), LRU_BLOCK ** -0.5),
        "l0_lru_ba": nrm((LRU_WIDTH,), 0.01),
        "l0_lru_wx": nrm((LRU_BLOCKS, LRU_BLOCK, LRU_BLOCK), LRU_BLOCK ** -0.5),
        "l0_lru_bx": nrm((LRU_WIDTH,), 0.01),
        "l0_lru_lambda": lam,
        "l0_cmp_pe_k": nrm((CMP_LEN, HEAD_DIM), 0.5),
        "l0_cmp_w1_k": nrm((CMP_LEN * HEAD_DIM, CMP_HIDDEN), (CMP_LEN * HEAD_DIM) ** -0.5),
        "l0_cmp_w2_k": nrm((CMP_HIDDEN, HEAD_DIM), CMP_HIDDEN ** -0.5),
        "l0_cmp_pe_v": nrm((CMP_LEN, HEAD_DIM), 0.5),
        "l0_cmp_w1_v": nrm((CMP_LEN * HEAD_DIM, CMP_HIDDEN), (CMP_LEN * HEAD_DIM) ** -0.5),
        "l0_cmp_w2_v": nrm((CMP_HIDDEN, HEAD_DIM), CMP_HIDDEN ** -0.5),
        "l0_w_out": nrm((MIX0, D), MIX0 ** -0.5),
        "l0_ffn_wg": nrm((D, D_FF), D ** -0.5),
        "l0_ffn_wu": nrm((D, D_FF), D ** -0.5),
        "l0_ffn_wd": nrm((D_FF, D), D_FF ** -0.5),
        "l1_norm_mix": gain(D),
        "l1_norm_ffn": gain(D),
        "l1_mod_w": nrm((D, 6 * D), 0.5 * D ** -0.5),
        "l1_mod_b": nrm((6 * D,), 0.01),
        "l1_w_in": nrm((D, IN1), D ** -0.5),
        "l1_w_out": nrm((MIX1, D), MIX1 ** -0.5),
        "l1_ffn_wg": nrm((D, D_FF), D ** -0.5),
        "l1_ffn_wu": nrm((D, D_FF), D ** -0.5),
        "l1_ffn_wd": nrm((D_FF, D), D_FF ** -0.5),
        "final_norm": gain(D),
    }

def first_block(x, c,
              l0_norm_mix, l0_norm_ffn, l0_mod_w, l0_mod_b, l0_w_in, l0_conv_w, l0_conv_b,
              l0_lru_wa, l0_lru_ba, l0_lru_wx, l0_lru_bx, l0_lru_lambda,
              l0_cmp_pe_k, l0_cmp_w1_k, l0_cmp_w2_k, l0_cmp_pe_v, l0_cmp_w1_v, l0_cmp_w2_v,
              l0_w_out, l0_ffn_wg, l0_ffn_wu, l0_ffn_wd,
              l1_norm_mix, l1_norm_ffn, l1_mod_w, l1_mod_b, l1_w_in, l1_w_out,
              l1_ffn_wg, l1_ffn_wu, l1_ffn_wd,
              final_norm):
    layer_params = [
        (l0_norm_mix, l0_norm_ffn, l0_mod_w, l0_mod_b, l0_w_in, l0_conv_w, l0_conv_b,
         l0_lru_wa, l0_lru_ba, l0_lru_wx, l0_lru_bx, l0_lru_lambda,
         l0_cmp_pe_k, l0_cmp_w1_k, l0_cmp_w2_k, l0_cmp_pe_v, l0_cmp_w1_v, l0_cmp_w2_v,
         l0_w_out, l0_ffn_wg, l0_ffn_wu, l0_ffn_wd),
        (l1_norm_mix, l1_norm_ffn, l1_mod_w, l1_mod_b, l1_w_in, l1_w_out,
         l1_ffn_wg, l1_ffn_wu, l1_ffn_wd),
    ]
    for layer in range(DEPTH):
        if layer % 2 == 0:
            x = layer_ab(x, c, *layer_params[layer])
        else:
            x = layer_c(x, c, *layer_params[layer])
    return rmsnorm(x, final_norm)


A_WIDTH = D_MODEL // 2
A_HEADS = A_WIDTH // HEAD_DIM
CHUNK = 128
B_WIDTH = D_MODEL // 2
CONV_WIDTH_2 = 31
IN_WIDTH = 2 * A_WIDTH + 2 * B_WIDTH
ATTN_HEADS = D_MODEL // HEAD_DIM
DILATED_PATTERNS = ((128, 1), (512, 4), (2048, 16))
BLOCK = 128
ROPE_THETA = 10000.0
D_FF_2 = 2816
FFN_CONV_WIDTH = 3
NEG = -1e30


def rms_norm(x, g):
    xf = x.astype(jnp.float32)
    y = xf * lax.rsqrt(jnp.mean(xf * xf, axis=-1, keepdims=True) + EPS)
    return (y * g.astype(jnp.float32)).astype(x.dtype)

def layer_norm(x, g, b):
    xf = x.astype(jnp.float32)
    mu = jnp.mean(xf, axis=-1, keepdims=True)
    var = jnp.mean(jnp.square(xf - mu), axis=-1, keepdims=True)
    y = (xf - mu) * lax.rsqrt(var + EPS)
    return (y * g.astype(jnp.float32) + b.astype(jnp.float32)).astype(x.dtype)

def causal_dwconv(x, w, b):
    k = w.shape[0]
    y = lax.conv_general_dilated(
        x, w[:, None, :].astype(x.dtype), window_strides=(1,),
        padding=[(k - 1, 0)], dimension_numbers=('NWC', 'WIO', 'NWC'),
        feature_group_count=x.shape[-1])
    return y + b.astype(x.dtype)

def rotary(x, pos):
    half = x.shape[-1] // 2
    inv = ROPE_THETA ** (-jnp.arange(half, dtype=jnp.float32) / half)
    ang = pos.astype(jnp.float32)[:, None] * inv[None, :]
    cos = jnp.cos(ang)[None, :, None, :]
    sin = jnp.sin(ang)[None, :, None, :]
    xf = x.astype(jnp.float32)
    x1, x2 = xf[..., :half], xf[..., half:]
    out = jnp.concatenate([x1 * cos - x2 * sin, x2 * cos + x1 * sin], axis=-1)
    return out.astype(x.dtype)

def chunked_spatial_gating(z, ln_g, ln_b, w_s, b_s):
    u, v = jnp.split(z, 2, axis=-1)
    v = layer_norm(v, ln_g, ln_b)
    bn, s, _ = v.shape
    v = v.reshape(bn, s // CHUNK, CHUNK, A_HEADS, HEAD_DIM)
    causal = jnp.tril(jnp.ones((CHUNK, CHUNK), dtype=bool))
    w = jnp.where(causal, w_s, jnp.zeros_like(w_s))
    mixed = jnp.einsum('hts,bcshd->bcthd', w, v) + b_s.T[None, None, :, :, None]
    return u * mixed.reshape(bn, s, A_WIDTH)

def conformer_conv(z, conv_w, conv_b, ln_g, ln_b):
    a, g = jnp.split(z, 2, axis=-1)
    h = a * jax.nn.sigmoid(g)
    h = causal_dwconv(h, conv_w, conv_b)
    h = layer_norm(h, ln_g, ln_b)
    return jax.nn.silu(h)

def dilated_branch(q, k, v, window, dilation):
    bn, s, h, dh = q.shape
    span = dilation * BLOCK
    s_pad = -(-s // span) * span
    seq_len = s_pad // dilation
    nb = seq_len // BLOCK
    reach = window // dilation

    def strided(t):
        t = jnp.pad(t, [(0, 0), (0, s_pad - s), (0, 0), (0, 0)])
        t = t.reshape(bn, seq_len, dilation, h, dh).transpose(0, 2, 1, 3, 4)
        return t.reshape(bn, dilation, nb, BLOCK, h, dh)

    def with_prev(t):
        prev = jnp.pad(t, [(0, 0), (0, 0), (1, 0), (0, 0), (0, 0), (0, 0)])[:, :, :-1]
        return jnp.concatenate([prev, t], axis=3)

    qs = strided(q)
    kw = with_prev(strided(k))
    vw = with_prev(strided(v))
    qi = jnp.arange(BLOCK)[:, None]
    kj = jnp.arange(2 * BLOCK)[None, :]
    dist = BLOCK + qi - kj
    band = (dist >= 0) & (dist <= reach)
    blk = jnp.arange(nb)[:, None, None]
    valid = band[None] & ((blk > 0) | (kj[None] >= BLOCK))

    scores = jnp.einsum('brnqhd,brnkhd->brnhqk', qs, kw).astype(jnp.float32)
    scores = scores * (HEAD_DIM ** -0.5)
    scores = jnp.where(valid[None, None, :, None], scores, NEG)
    m = jnp.max(scores, axis=-1, keepdims=True)
    p = jnp.exp(scores - m)
    l = jnp.sum(p, axis=-1, keepdims=True)
    o = jnp.einsum('brnhqk,brnkhd->brnqhd', p / l, vw.astype(jnp.float32))
    lse = (m + jnp.log(l))[..., 0]

    o = o.reshape(bn, dilation, seq_len, h, dh).transpose(0, 2, 1, 3, 4)
    o = o.reshape(bn, s_pad, h, dh)[:, :s]
    lse = lse.transpose(0, 1, 2, 4, 3).reshape(bn, dilation, seq_len, h)
    lse = lse.transpose(0, 2, 1, 3).reshape(bn, s_pad, h)[:, :s]
    return o, lse

def dilated_attention(q, k, v):
    outs, lses = [], []
    for window, dilation in DILATED_PATTERNS:
        o, lse = dilated_branch(q, k, v, window, dilation)
        outs.append(o)
        lses.append(lse)
    wts = jax.nn.softmax(jnp.stack(lses, axis=0), axis=0)
    return jnp.einsum('pbsh,pbshd->bshd', wts, jnp.stack(outs, axis=0))

def conv_ffn(x, norm_g, w_up, conv_w, conv_b, w_down):
    h = rms_norm(x, norm_g)
    u = causal_dwconv(h @ w_up, conv_w, conv_b)
    gate, val = jnp.split(u, 2, axis=-1)
    return x + (jax.nn.silu(gate) * val) @ w_down

def second_inputs(seed: int = 0) -> dict:
    key = jax.random.key(seed)
    keys = iter(jax.random.split(key, 32))
    n_even = (DEPTH + 1) // 2
    n_odd = DEPTH // 2
    f32 = jnp.float32

    def nrm(shape, scale):
        return jax.random.normal(next(keys), shape, f32) * scale

    def gain(shape):
        return 1.0 + nrm(shape, 0.02)

    return {
        'x': nrm((BATCH, SEQ, D_MODEL), 1.0),
        'even_norm_g': gain((n_even, D_MODEL)),
        'even_w_in': nrm((n_even, D_MODEL, IN_WIDTH), D_MODEL ** -0.5),
        'even_b_in': nrm((n_even, IN_WIDTH), 0.02),
        'even_v_ln_g': gain((n_even, A_WIDTH)),
        'even_v_ln_b': nrm((n_even, A_WIDTH), 0.02),
        'even_w_s': nrm((n_even, A_HEADS, CHUNK, CHUNK), CHUNK ** -0.5),
        'even_b_s': gain((n_even, A_HEADS, CHUNK)),
        'even_conv_w': nrm((n_even, CONV_WIDTH_2, B_WIDTH), CONV_WIDTH_2 ** -0.5),
        'even_conv_b': nrm((n_even, B_WIDTH), 0.02),
        'even_conv_ln_g': gain((n_even, B_WIDTH)),
        'even_conv_ln_b': nrm((n_even, B_WIDTH), 0.02),
        'even_w_out': nrm((n_even, A_WIDTH + B_WIDTH, D_MODEL), (A_WIDTH + B_WIDTH) ** -0.5),
        'odd_norm_g': gain((n_odd, D_MODEL)),
        'odd_w_qkv': nrm((n_odd, D_MODEL, 3 * D_MODEL), D_MODEL ** -0.5),
        'odd_w_o': nrm((n_odd, D_MODEL, D_MODEL), D_MODEL ** -0.5),
        'ffn_norm_g': gain((DEPTH, D_MODEL)),
        'ffn_w_up': nrm((DEPTH, D_MODEL, 2 * D_FF_2), D_MODEL ** -0.5),
        'ffn_conv_w': nrm((DEPTH, FFN_CONV_WIDTH, 2 * D_FF_2), FFN_CONV_WIDTH ** -0.5),
        'ffn_conv_b': nrm((DEPTH, 2 * D_FF_2), 0.02),
        'ffn_w_down': nrm((DEPTH, D_FF_2, D_MODEL), D_FF_2 ** -0.5),
        'final_norm_g': gain((D_MODEL,)),
    }

def second_block(x, even_norm_g, even_w_in, even_b_in, even_v_ln_g, even_v_ln_b,
              even_w_s, even_b_s, even_conv_w, even_conv_b, even_conv_ln_g,
              even_conv_ln_b, even_w_out, odd_norm_g, odd_w_qkv, odd_w_o,
              ffn_norm_g, ffn_w_up, ffn_conv_w, ffn_conv_b, ffn_w_down,
              final_norm_g):
    bn, s, _ = x.shape
    pos = jnp.arange(s)
    for i in range(DEPTH):
        j = i // 2
        if i % 2 == 0:
            h = rms_norm(x, even_norm_g[j])
            z = h @ even_w_in[j] + even_b_in[j]
            za = jax.nn.gelu(z[..., :2 * A_WIDTH])
            zb = z[..., 2 * A_WIDTH:]
            ya = chunked_spatial_gating(za, even_v_ln_g[j], even_v_ln_b[j],
                                        even_w_s[j], even_b_s[j])
            yb = conformer_conv(zb, even_conv_w[j], even_conv_b[j],
                                even_conv_ln_g[j], even_conv_ln_b[j])
            x = x + jnp.concatenate([ya, yb], axis=-1) @ even_w_out[j]
        else:
            h = rms_norm(x, odd_norm_g[j])
            qkv = (h @ odd_w_qkv[j]).reshape(bn, s, 3, ATTN_HEADS, HEAD_DIM)
            q = rotary(qkv[:, :, 0], pos)
            k = rotary(qkv[:, :, 1], pos)
            v = qkv[:, :, 2]
            o = dilated_attention(q, k, v).astype(x.dtype).reshape(bn, s, D_MODEL)
            x = x + o @ odd_w_o[j]
        x = conv_ffn(x, ffn_norm_g[i], ffn_w_up[i], ffn_conv_w[i], ffn_conv_b[i],
                     ffn_w_down[i])
    return rms_norm(x, final_norm_g)


def setup_inputs(seed=0):
    out = dict(first_inputs(seed))
    for name, value in second_inputs(seed + 1).items():
        if name != "x":
            out[name + "_2"] = value
    return out


def reference(
    x, c, l0_norm_mix, l0_norm_ffn, l0_mod_w, l0_mod_b, l0_w_in, l0_conv_w, l0_conv_b,
    l0_lru_wa, l0_lru_ba, l0_lru_wx, l0_lru_bx, l0_lru_lambda, l0_cmp_pe_k, l0_cmp_w1_k,
    l0_cmp_w2_k, l0_cmp_pe_v, l0_cmp_w1_v, l0_cmp_w2_v, l0_w_out, l0_ffn_wg, l0_ffn_wu,
    l0_ffn_wd, l1_norm_mix, l1_norm_ffn, l1_mod_w, l1_mod_b, l1_w_in, l1_w_out, l1_ffn_wg,
    l1_ffn_wu, l1_ffn_wd, final_norm, even_norm_g_2, even_w_in_2, even_b_in_2, even_v_ln_g_2,
    even_v_ln_b_2, even_w_s_2, even_b_s_2, even_conv_w_2, even_conv_b_2, even_conv_ln_g_2,
    even_conv_ln_b_2, even_w_out_2, odd_norm_g_2, odd_w_qkv_2, odd_w_o_2, ffn_norm_g_2,
    ffn_w_up_2, ffn_conv_w_2, ffn_conv_b_2, ffn_w_down_2, final_norm_g_2,
):
    x = first_block(
        x, c, l0_norm_mix, l0_norm_ffn, l0_mod_w, l0_mod_b, l0_w_in, l0_conv_w, l0_conv_b,
        l0_lru_wa, l0_lru_ba, l0_lru_wx, l0_lru_bx, l0_lru_lambda, l0_cmp_pe_k, l0_cmp_w1_k,
        l0_cmp_w2_k, l0_cmp_pe_v, l0_cmp_w1_v, l0_cmp_w2_v, l0_w_out, l0_ffn_wg, l0_ffn_wu,
        l0_ffn_wd, l1_norm_mix, l1_norm_ffn, l1_mod_w, l1_mod_b, l1_w_in, l1_w_out, l1_ffn_wg,
        l1_ffn_wu, l1_ffn_wd, final_norm,
    )
    return second_block(
        x, even_norm_g_2, even_w_in_2, even_b_in_2, even_v_ln_g_2, even_v_ln_b_2, even_w_s_2,
        even_b_s_2, even_conv_w_2, even_conv_b_2, even_conv_ln_g_2, even_conv_ln_b_2,
        even_w_out_2, odd_norm_g_2, odd_w_qkv_2, odd_w_o_2, ffn_norm_g_2, ffn_w_up_2,
        ffn_conv_w_2, ffn_conv_b_2, ffn_w_down_2, final_norm_g_2,
    )


_drawn_inputs = setup_inputs


def setup_inputs(seed=0):
    import zlib

    import numpy as np

    out = dict(_drawn_inputs(seed))
    spreads = {}
    factors = {'l0_norm_mix': 3.32,
     'l0_norm_ffn': 2.95,
     'l0_mod_b': 2.993,
     'l0_conv_b': 4.936,
     'l0_lru_ba': 8.0,
     'l0_lru_bx': 8.0,
     'l0_cmp_pe_k': 7.447,
     'l0_cmp_w1_k': 2.783,
     'l0_cmp_w2_k': 2.684,
     'l1_norm_mix': 3.877,
     'l1_norm_ffn': 2.92,
     'l1_mod_b': 4.042,
     'even_norm_g_2': 3.423,
     'even_b_in_2': 3.221,
     'even_v_ln_g_2': 8.0,
     'even_v_ln_b_2': 8.0,
     'even_b_s_2': 6.364,
     'even_conv_b_2': 3.26,
     'even_conv_ln_g_2': 16.002,
     'even_conv_ln_b_2': 16.433,
     'odd_norm_g_2': 8.0,
     'ffn_norm_g_2': 3.054,
     'ffn_conv_b_2': 3.133,
     'final_norm_g_2': 8.092}
    for name, (base, spread) in spreads.items():
        noise = np.random.default_rng([zlib.crc32(name.encode()), seed]).standard_normal(out[name].shape)
        drawn = base * np.exp(spread * noise) if base else spread * noise
        out[name] = jnp.asarray(drawn.astype(out[name].dtype))
    for name, factor in factors.items():
        out[name] = (out[name] * factor).astype(out[name].dtype)
    return out
```

```python
from contextlib import ExitStack

import numpy as np

import concourse.bass as bass
from concourse import mybir

F32 = mybir.dt.float32
F32R = mybir.dt.float32r
ALU = mybir.AluOpType
ACT = mybir.ActivationFunctionType
AX_X = mybir.AxisListType.X

P = 128
D = 1024
T = 512
KB = D // P
QB = T // P
HD = 64
SCALE = HD ** -0.5
EPS = 1e-6
NEG = -1e30
TAKEN = -3e38
FF = 2816
FC = FF // P
PARTS = (8, 8, 6)
LRU = 512
LC = LRU // P
CMP_LEN, CMP_STRIDE, NCMP = 32, 16, (T - 32) // 16 + 1
TOPK = 128
IDX_HEADS = 8
TAPS_LRU, TAPS_CONV, TAPS_FFN = 4, 31, 3
RING = 4
LRU_C = 8.0
IDX_SCALE = HD ** -0.5
LOWEST = -3e38
MRING = 2
SUMS = 4
AHEAD = 2

FFN_PANELS = 2 * FC + KB * len(PARTS)
P_AX = 0
P_AGATE = P_AX + LC
P_Q0 = P_AGATE + LC
P_KC, P_VC, P_KS, P_KW, P_VS, P_VW = range(P_Q0 + 4, P_Q0 + 10)
P_OUT0 = P_VW + 1
P_FFN0 = P_OUT0 + KB
P_QI = P_FFN0 + FFN_PANELS
P_V1 = P_QI + 4
P_KI = P_V1 + 2
P_Q1 = P_KI + 1
P_K1 = P_Q1 + KB
P_OUT1 = P_K1 + 1
P_FFN1 = P_OUT1 + KB
P_AG = P_FFN1 + FFN_PANELS
P_U = P_AG + 8
P_V2 = P_U + 4
P_OUT2 = P_V2 + 4
P_FFN2 = P_OUT2 + KB
P_Q3 = P_FFN2 + FFN_PANELS
P_K3 = P_Q3 + KB
P_V3 = P_K3 + KB
P_OUT3 = P_V3 + KB
P_FFN3 = P_OUT3 + KB
N_PANELS = P_FFN3 + FFN_PANELS
assert all(p % 2 == 0 for p in (P_VS, P_V1, P_V2, P_V3))

MOD = 6 * KB
MOD_FIRST = 2 * KB
MOD_TWICE = 6
MOD_UNTIL = MOD_TWICE + (2 * MOD - MOD_FIRST - 2 * MOD_TWICE)


ALONE = [q for q in range(MOD_FIRST) if q % 8 in (3, 6, 7)]


def summed(q):
    return q + 1 - sum(a <= q for a in ALONE)


def mods_beside(p):
    if p < MOD_TWICE:
        return [MOD_FIRST + 2 * p, MOD_FIRST + 2 * p + 1]
    return [MOD_FIRST + MOD_TWICE + p] if p < MOD_UNTIL else []


COLS = {}
_at = 0
for _name, _n in [
    ("c", KB), ("g0mix", KB), ("g0ffn", KB), ("g1mix", KB), ("g1ffn", KB), ("modb", 2 * MOD),
    ("lconv", TAPS_LRU * LC), ("lconvb", LC), ("ba", LC), ("bx", LC), ("lam", LC),
    ("final1", KB), ("even", KB), ("bu", 4), ("bga", 4), ("bgg", 4), ("cconv", TAPS_CONV * 4), ("cconvb", 4),
    ("clng", 4), ("clnb", 4), ("odd", KB), ("ffn2", KB), ("ffn3", KB),
    ("fw2", TAPS_FFN * 2 * FC), ("fb2", 2 * FC), ("fw3", TAPS_FFN * 2 * FC), ("fb3", 2 * FC), ("final2", KB),
]:
    COLS[_name] = _at
    _at += _n
N_COLS = _at


def build(nc, A):
    with ExitStack() as ctx:
        base = (nc.sbuf_base + 63) // 64 * 64
        place = [base]

        def sb(name, shape, dt=F32, at=None):
            size = int(np.prod(shape[1:])) * 4
            where = place[0] if at is None else at
            if at is None:
                place[0] += (size + 63) // 64 * 64
            return nc.alloc_sbuf_tensor_at(name, list(shape), dt, offset=where)

        def sem(name):
            return ctx.enter_context(nc.semaphore(name))

        bank = [ctx.enter_context(nc.psum_tensor(f"bank{n}", [P, 512], F32)) for n in range(8)]
        MODBANK = bank[7]

        x = sb("x", [P, KB, T])
        hx = place[0]
        h_hi = sb("h_hi", [P, KB, T], F32R)
        h_lo = sb("h_lo", [P, KB, T], F32R)
        raw = sb("raw", [P, RING, KB * P])
        mx = place[0] + 2 * RING * KB * P * 4
        w_hi = sb("w_hi", [P, RING, KB * P], F32R)
        w_lo = sb("w_lo", [P, RING, KB * P], F32R)
        assert place[0] == mx
        modraw = sb("modraw", [P, MRING, KB * P])
        modsum = sb("modsum", [P, SUMS, P])
        cols = sb("cols", [P, N_COLS])
        ident = sb("ident", [P, P])
        ones = sb("ones", [P, P])
        swap = sb("swap", [P, P])
        modv = sb("modv", [P, 2 * MOD])
        gains = sb("gains", [P, 4 * KB])
        plain = sb("plain", [P, 2])
        own_half = sb("own_half", [P, 2])
        csil = sb("csil", [P, KB])
        root = sb("root", [P, 2 * QB])
        mask = sb("mask", [P, QB, T])
        cmask = sb("cmask", [P, QB, 32])
        stat = sb("stat", [P, 3, 64])
        w_small = sb("w_small", [P, KB, 24])
        small = sb("small", [P, QB, 24])
        gx = place[0]
        g_hi = sb("g_hi", [P, KB, T], F32R)
        g_lo = sb("g_lo", [P, KB, T], F32R)
        vx = place[0]
        place[0] += 24 * 1024
        sx = place[0]
        place[0] += 24 * 1024
        assert place[0] <= nc.sbuf_usable_end

        def g(name, shape, kib, dt=F32):
            return sb(name, shape, dt, at=gx + int(kib * 1024))

        def v(name, shape, kib):
            return sb(name, shape, at=vx + int(kib * 1024))

        def s(name, shape, kib):
            return sb(name, shape, at=sx + int(kib * 1024))

        first_mods = [sb(f"first_mods{n}", [P, 4, KB * P], at=at)
                      for n, at in enumerate((hx, hx + 16 * 1024, gx, gx + 16 * 1024))]
        sq = s("sq", [P, 2, T], 0)
        acc = s("acc", [P, T], 4)
        diag = s("diag", [P, QB, P], 6)
        tn = s("tn", [P, 2, T], 8)
        silu = s("silu", [P, 2, T], 12)
        prod = s("prod", [P, 2, T], 16)
        cval = s("cval", [P, T], 20)
        cgate = s("cgate", [P, 2, T], 0)
        yout = g("yout", [P, KB, T], 0)
        orow = s("orow", [P, QB, 512], 0)
        orow2 = v("orow2", [P, QB, D], 16)
        srow = s("srow", [P, 2, T], 8)
        prob = s("prob", [P, 3, T], 12)
        probT = s("probT", [P, 2, T], 18)
        axp = g("axp", [P, LC, T + 3], 0)
        ya = g("ya", [P, LC, T], 8.25)
        q0 = g("q0", [P, 4, T], 16.25)
        kcT = g("kcT", [P, T], 24.25)
        vcT = g("vcT", [P, T], 26.25)
        ksT = g("ksT", [P, T], 28.25)
        w1 = v("w1", [P, CMP_LEN, P], 0)
        kwT = v("kwT", [P, T], 16)
        w2 = v("w2", [P, 2, HD], 18)
        peT = v("peT", [P, 2, CMP_LEN], 18.5)
        hid = v("hid", [P, 2, 64], 18.75)
        kdiag = v("kdiag", [P, 64], 19.25)
        vtok0 = v("vtok0", [P, QB, 256], 20)
        k0pad = v("k0pad", [P, 2, 2, T], 0)
        lruw = s("lruw", [P, 2, LC, P], 0)
        xc = s("xc", [P, LC, T], 4)
        inp = s("inp", [P, LC, T], 12)
        rt = axp
        decay = s("decay", [P, 2, T], 20)
        sp = sb("sp", [P, 6, LC])
        blocks = s("blocks", [P, 2, CMP_LEN, 64], 0)
        cprob = s("cprob", [P, QB, 8, 32], 8)
        cst = s("cst", [P, 4, QB, 8], 12)
        cpT = s("cpT", [P, 2, QB, P], 16)
        vdiag = s("vdiag", [P, 4, HD], 20)
        q1 = g("q1", [P, KB, T], 0)
        qi = g("qi", [P, 4, T], 16)
        kiT = g("kiT", [P, T], 24)
        k1pad = sb("k1pad", [P, 2, T], at=mx)
        v1t = g("v1t", [P, QB, P], 28)
        iacc = v("iacc", [P, QB - 1, T], 0)
        irel = v("irel", [P, 2, T], 6)
        top8 = v("top8", [P, 3, 8], 10)
        pad = g("pad", [P, 4, TAPS_CONV - 1 + T], 0)
        cout = g("cout", [P, 4, T], 8.5)
        u2 = g("u2", [P, 4, T], 16.5)
        v2t = v("v2t", [P, QB, 512], 0)
        wsT = v("wsT", [P, 8, P], 8)
        rows = v("rows", [P, 3, 512], 12)
        bs = v("bs", [P, 4, P], 18)
        lnst = v("lnst", [P, QB, 16], 20)
        sg = s("sg", [P, 2, T], 12)
        tapped = s("tapped", [P, 2, T], 20)
        ysp = s("ysp", [P, 2, T], 16)
        q3 = g("q3", [P, KB, T], 0)
        k3 = g("k3", [P, KB, T], 16)
        v3t = v("v3t", [P, QB, D], 0)
        k3pad = sb("k3pad", [P, 2, 2, T], at=mx)
        rope = v("rope", [P, 2, T], 16)
        rot = s("rot", [P, 2, T], 0)
        rot2 = s("rot2", [P, T], 4)

        raw_landed = [sem(f"raw_landed{n}") for n in range(RING)]
        mod_landed = [sem(f"mod_landed{n}") for n in range(MRING)]
        first_landed = [sem(f"first_landed{n}") for n in range(MOD_FIRST // 4)]
        consts_landed = sem("consts_landed")
        x_landed = sem("x_landed")
        lru_landed = sem("lru_landed")
        w1_landed = sem("w1_landed")
        masks_landed = sem("masks_landed")
        layer2_landed = sem("layer2_landed")
        rope_landed = sem("rope_landed")
        small_landed = sem("small_landed")
        filled = sem("filled")
        hi_ready = sem("hi_ready")
        lo_ready = sem("lo_ready")
        panel_done = sem("panel_done")
        bank_free = sem("bank_free")
        mod_summed = sem("mod_summed")
        mod_used = sem("mod_used")
        csil_ready = sem("csil_ready")
        squares_ready = sem("squares_ready")
        squares_added = sem("squares_added")
        acc_ready = sem("acc_ready")
        sums_ready = sem("sums_ready")
        root_ready = sem("root_ready")
        diag_ready = sem("diag_ready")
        rstd_ready = sem("rstd_ready")
        t_ready = sem("t_ready")
        h_hi_ready = sem("h_hi_ready")
        h_lo_ready = sem("h_lo_ready")
        x_norm = sem("x_norm")
        yout_ready = sem("yout_ready")
        yout_stored = sem("yout_stored")
        silu_ready = sem("silu_ready")
        cgate_ready = sem("cgate_ready")
        prod_ready = sem("prod_ready")
        f_hi_ready = sem("f_hi_ready")
        f_lo_ready = sem("f_lo_ready")
        score_ready = sem("score_ready")
        keys_padded = sem("keys_padded")
        masked_ready = sem("masked_ready")
        exp_ready = sem("exp_ready")
        pt_done = sem("pt_done")
        pt_copied = sem("pt_copied")
        pv_done = sem("pv_done")
        o_done = sem("o_done")
        ot_done = sem("ot_done")
        ot_hi = sem("ot_hi")
        ot_lo = sem("ot_lo")
        spexp = sem("spexp")
        conv_ready = sem("conv_ready")
        lgate_done = sem("lgate_done")
        lsig_ready = sem("lsig_ready")
        ltanh_ready = sem("ltanh_ready")
        lsqrt_ready = sem("lsqrt_ready")
        ldecay_ready = sem("ldecay_ready")
        agelu_ready = sem("agelu_ready")
        y_ready = sem("y_ready")
        y_hi = sem("y_hi")
        y_lo = sem("y_lo")
        hid_done = sem("hid_done")
        blocks_ready = sem("blocks_ready")
        hid_ready = sem("hid_ready")
        cmp_done = sem("cmp_done")
        cmp_ready = sem("cmp_ready")
        gate_done = sem("gate_done")
        gate_ready = sem("gate_ready")
        cs_done = sem("cs_done")
        cmax_ready = sem("cmax_ready")
        cexp_ready = sem("cexp_ready")
        cpt_done = sem("cpt_done")
        cpt_copied = sem("cpt_copied")
        cpv_done = sem("cpv_done")
        co_done = sem("co_done")
        idx_done = sem("idx_done")
        relu_ready = sem("relu_ready")
        idx_added = sem("idx_added")
        ws_masked = sem("ws_masked")
        pad_ready = sem("pad_ready")
        tap_made = sem("tap_made")
        tap_added = sem("tap_added")
        sg_ready = sem("sg_ready")
        bias_added = sem("bias_added")
        u_ready = sem("u_ready")
        v_gelu = sem("v_gelu")
        var_ready = sem("var_ready")
        vstd_ready = sem("vstd_ready")
        vln_ready = sem("vln_ready")
        mix_done = sem("mix_done")
        mean_acc = sem("mean_acc")
        mean_done = sem("mean_done")
        centred = sem("centred")
        cn_ready = sem("cn_ready")
        csilu_ready = sem("csilu_ready")
        rot_copied = sem("rot_copied")
        swap_done = sem("swap_done")
        rot_done = sem("rot_done")

        def taps_beside(p):
            return range(1 + 2 * (p - P_U), 3 + 2 * (p - P_U))

        DVE_TAPS3 = taps_beside(P_OUT2)[0]

        block = ctx.enter_context(nc.Block())

        def col(name, n=0):
            at = COLS[name] + n
            return cols[:, at:at + 1]

        one, zero = plain[:, 0:1], plain[:, 1:2]

        H_OF = {0: 0, 1: 1, 2: 2, 3: 3, 5: 4, 7: 5, 8: 6, 9: 7}
        SQ_AT = [KB * r if r <= 6 else KB * r - 4 for r in range(12)]

        def gain(r, k):
            if r < 4:
                return gains[:, r * KB + k:r * KB + k + 1]
            return col({4: "final1", 5: "even", 7: "ffn2", 8: "odd", 9: "ffn3", 10: "final2"}[r], k)

        def shift(r, k):
            if r < 4:
                at = (r // 2) * MOD + (0 if r % 2 == 0 else 3 * KB) + k
                return modv[:, at:at + 1]
            return zero

        def out_gate(layer, ffn, n):
            if layer < 2:
                at = layer * MOD + (5 if ffn else 2) * KB + n
                return modv[:, at:at + 1]
            return one

        TURNS = ((QB - 1, 0), (QB - 2, 1))
        UNITS0 = [(i, c, b, br) for both in TURNS for br in (1, 2) for c in range(4) for b in range(2) for i in both]
        UNITS1 = [(i, c, b, 0) for both in TURNS for c in range(KB) for b in range(2) for i in both]
        U_AT = [0, len(UNITS0), len(UNITS0) + len(UNITS1)]

        def q_of(run, unit):
            i, c, _, _ = unit
            return (q0, q1, q3)[run][:, c, P * i:P * i + P]

        def pair_at(unit):
            i, c, _, _ = unit
            return KB * (i not in TURNS[0]) + c

        def k_of(run, unit):
            i, c, b, br = unit
            n = P * (i + 1)
            if run == 0:
                return k0pad[:, br - 1, b, 0:n]
            return k1pad[:, b, 0:n] if run == 1 else k3pad[:, pair_at(unit) % 2, b, 0:n]

        def head_of(run, unit):
            _, c, b, _ = unit
            return (c + 4 * b, c + KB * b, 2 * c + b)[run]

        def v_of(run, unit, j):
            _, c, b, br = unit
            if run == 0:
                return vtok0[:, j, P * (br - 1) + HD * b:P * (br - 1) + HD * b + HD]
            if run == 1:
                return v1t[:, j, HD * b:HD * b + HD]
            at = HD * head_of(run, unit)
            return v3t[:, j, at:at + HD]

        def o_of(run, unit):
            i, at = unit[0], HD * head_of(run, unit)
            return (orow if run == 0 else orow2)[:, i, at:at + HD]

        def block_out(run, i, f):
            return (orow if run == 0 else orow2)[:, i, P * f:P * f + P]

        ROUNDS = 2
        OT_WIDE = [2, 4, 4]
        OT_AT = [0, ROUNDS * QB, 2 * ROUNDS * QB]
        FIRST_OUT = [4, 0, 0]

        def turned(run):
            return MODBANK[:, 512 - P * OT_WIDE[run]:512]

        def rounds_at(n):
            out, half = [], len(UNITS1) // 2
            for turn_, both in enumerate(TURNS):
                for m, (i, r) in enumerate([(i, r) for i in both for r in range(ROUNDS)]):
                    when = half + 5 + 4 * m if turn_ == 0 else len(UNITS1)
                    if when == n:
                        out.append((2 * ROUNDS * turn_ + m, i, r))
            return out

        def done_for(m):
            return len(UNITS1) // 2 if m < 2 * ROUNDS else len(UNITS1)

        SBANK = (0, 1, 6)

        @block.sync
        def _(sp_):
            def load_raw(p, slot=None, after=None):
                if after is not None:
                    sp_.wait_ge(lo_ready, after)
                sp_.dma_start(raw[:, p % RING if slot is None else slot, :], A["panels"][p])\
                    .then_inc(raw_landed[p % RING if slot is None else slot], 16)

            def load_mod(q, slot, after=None):
                if after is not None:
                    sp_.wait_ge(mod_summed, after)
                sp_.dma_start(modraw[:, slot, :], A["mods"][q]).then_inc(mod_landed[slot], 16)

            sp_.dma_start(cols[:, :], A["cols"]).then_inc(consts_landed, 16)
            sp_.dma_start(x[:, :, :], A["x"]).then_inc(x_landed, 16)
            for n in range(MOD_FIRST // 4):
                sp_.dma_start(first_mods[n][:, :, :], A["mods"][4 * n:4 * n + 4].rearrange("n p k -> p n k"))\
                    .then_inc(first_landed[n], 16)
            for p in range(RING):
                load_raw(p)
            for q in range(MOD_FIRST, MOD_FIRST + MRING):
                load_mod(q, q % MRING)
            for p in range(MOD_TWICE):
                load_raw(p + RING, after=p + 1)
                for q in mods_beside(p):
                    if q >= MOD_FIRST + MRING:
                        load_mod(q, q % MRING, summed(q - MRING))
            q_first, n = mods_beside(MOD_TWICE)[0], (MOD_UNTIL - MOD_TWICE) // 4
            with sp_.Fori(0, n) as it:
                for j in range(4):
                    p = MOD_TWICE + j
                    load_raw(it * 4 + (p + RING), (p + RING) % RING, it * 4 + (p + 1))
                    load_mod(it * 4 + (q_first + j), (q_first + j) % MRING, it * 4 + summed(q_first + j - MRING))
            p_first = MOD_UNTIL + RING
            n = (N_PANELS - p_first) // 4
            with sp_.Fori(0, n) as it:
                for j in range(4):
                    load_raw(it * 4 + (p_first + j), (p_first + j) % RING, it * 4 + (p_first + j - RING + 1))
            for p in range(p_first + 4 * n, N_PANELS):
                load_raw(p, after=p - RING + 1)

        @block.gpsimd
        def _(pool):
            def split_lo(p, slot):
                pool.wait_ge(hi_ready, p + 1)
                pool.tensor_tensor(w_lo[:, slot, :], raw[:, slot, :], w_hi[:, slot, :].bitcast(F32), ALU.subtract)\
                    .then_inc(lo_ready, 1)

            def split_from(p0, n):
                with pool.Fori(0, n // RING) as it:
                    for j in range(RING):
                        split_lo(it * RING + (p0 + j), (p0 + j) % RING)
                for p in range(p0 + n // RING * RING, p0 + n):
                    split_lo(p, p % RING)

            split_from(0, P_OUT0 + RING)
            pool.wait_ge(cmp_done, 2)
            pool.wait_ge(bank_free, P_OUT0)
            for br, src in enumerate((ksT, kwT)):
                for b in range(2):
                    pool.tensor_scalar(k0pad[:, br, b, :], src[:, :], own_half[:, b:b + 1], None, ALU.mult)
            pool.drain()
            pool.sem_inc(keys_padded, 1)
            split_from(P_OUT0 + RING, P_AG - P_OUT0 - RING)
            pool.wait_ge(layer2_landed, 48)
            pool.affine_select(out=wsT[:, :, :], in_=wsT[:, :, :], compare_op=ALU.is_ge, fill=0.0, base=0,
                               pattern=[[0, 8], [1, P]], channel_multiplier=-1).then_inc(ws_masked, 1)
            split_from(P_AG, P_U + RING - P_AG)
            for p in range(P_U + RING, P_OUT2 + RING):
                split_lo(p, p % RING)
                for k in taps_beside(p - RING):
                    pool.wait_ge(tap_made, k)
                    pool.tensor_tensor(cout[:, 3, :], cout[:, 3, :], tapped[:, k % 2, :], ALU.add).then_inc(tap_added, 1)
                    pool.drain()
            split_from(P_OUT2 + RING, P_OUT3 - P_OUT2)
            pool.wait_ge(bank_free, P_OUT3)
            for g_ in range(2 * KB):
                if g_ >= 2:
                    pool.wait_ge(score_ready, U_AT[2] + 4 * (g_ - 1))
                for b in range(2):
                    pool.tensor_scalar(k3pad[:, g_ % 2, b, :], k3[:, g_ % KB, :], own_half[:, b:b + 1], None, ALU.mult)
                pool.drain()
                pool.sem_inc(keys_padded, 1)
            split_from(P_OUT3 + RING, N_PANELS - P_OUT3 - RING)

        @block.tensor
        def _(pe):
            def three(out, w_h, w_l, m_h, m_l, start, stop):
                pe.matmul(out, w_h, m_h, start=start, stop=False)
                pe.matmul(out, w_h, m_l, start=False, stop=False)
                return pe.matmul(out, w_l, m_h, start=False, stop=stop)

            def first_mod_alone(q):
                pe.wait_ge(first_landed[q // 4], 16)
                for k in range(KB):
                    m = pe.matmul(mod_column(q), first_mods[q // 4][:, q % 4, P * k:P * k + P], csil[:, k:k + 1],
                                  start=(k == 0), stop=(k == KB - 1))
                m.then_inc(mod_used, 1)

            def mod_panel(slot, summed, out):
                pe.wait_ge(mod_summed, summed)
                pe.matmul(out, modsum[:, slot, :], ones[:, 0:1], start=True, stop=True).then_inc(mod_used, 1)

            def mod_column(q):
                return MODBANK[:, 0:2 * MOD].rearrange("p (n o) -> p n o", o=1)[:, q, :]

            def panel(p, slot, m_hi, m_lo, nk=KB, moving=None):
                pe.wait_ge(lo_ready, p + 1)
                if not isinstance(p, int) or p >= RING:
                    pe.wait_ge(bank_free, p - RING + 1)
                for k in range(nk):
                    if moving is not None:
                        pe.wait_ge(moving[0], moving[1] + k + 1)
                    wh, wl = w_hi[:, slot, P * k:P * k + P], w_lo[:, slot, P * k:P * k + P]
                    m = three(bank[slot][:, :], wh, wl, m_hi[:, k, :], m_lo[:, k, :], k == 0, k == nk - 1)
                m.then_inc(panel_done, 1)

            def token_panels(p):
                pe.wait_ge(lo_ready, p + 2)
                pe.wait_ge(bank_free, p - RING + 2)
                slot = p % RING
                for j in range(QB):
                    out = bank[slot + j // 2][:, 2 * P * (j % 2):2 * P * (j % 2) + 2 * P]
                    for k in range(KB):
                        wh, wl = w_hi[:, slot:slot + 2, P * k:P * k + P], w_lo[:, slot:slot + 2, P * k:P * k + P]
                        th, tl = h_hi[:, k, P * j:P * j + P], h_lo[:, k, P * j:P * j + P]
                        m = three(out, th, tl, wh, wl, k == 0, k == KB - 1)
                m.then_inc(panel_done, 2)

            def panels(p0, n, m_hi, m_lo, nk=KB, moving=None, mods=False):
                with pe.Fori(0, n // 4) as it:
                    for j in range(4):
                        panel(it * 4 + (p0 + j), (p0 + j) % RING, m_hi, m_lo, nk, moving if j == 0 else None)
                        if mods:
                            q = mods_beside(p0)[0] + j
                            mod_panel(summed(q) % SUMS, it * 4 + summed(q), mod_column(it * 4 + q))
                for p in range(p0 + n // 4 * 4, p0 + n):
                    panel(p, p % RING, m_hi, m_lo, nk)

            def with_mods(p):
                for q in mods_beside(p):
                    mod_panel(summed(q) % SUMS, summed(q), mod_column(q))

            def rstd(r):
                pe.wait_ge(acc_ready, r + 1)
                for j in range(QB):
                    m = pe.matmul(bank[4][:, j:j + 1], acc[:, P * j:P * j + P], ones[:, 0:1], start=True, stop=True)
                m.then_inc(sums_ready, 1)
                pe.wait_ge(diag_ready, r + 1)
                for j in range(QB):
                    m = pe.matmul(bank[5][:, P * j:P * j + P], ones[:, :], diag[:, j, :], start=True, stop=True)
                m.then_inc(rstd_ready, 1)

            def ffn(layer, p0, r):
                f, p = FC * layer, p0
                for n, size in enumerate(PARTS):
                    panels(p, 2 * size, h_hi, h_lo, moving=(h_lo_ready, KB * H_OF[r]) if n == 0 else None,
                           mods=p < MOD_UNTIL)
                    p += 2 * size
                    panels(p, KB, g_hi, g_lo, size, moving=(f_lo_ready, f), mods=p < MOD_UNTIL)
                    p += KB
                    f += size

            def attention(run):
                units, at = (UNITS0, UNITS1, UNITS1)[run], U_AT[run]

                def scores(n):
                    if n >= 3:
                        pe.wait_ge(masked_ready, at + n - 2)
                    if run == 2 and n % 4 == 0:
                        pe.wait_ge(keys_padded, 2 + pair_at(units[n]))
                    w = P * (units[n][0] + 1)
                    pe.matmul(bank[SBANK[n % 3]][:, 0:w], q_of(run, units[n]), k_of(run, units[n]), start=True, stop=True)\
                        .then_inc(score_ready, 1)

                def turn(n):
                    pe.wait_ge(exp_ready, at + n + 1)
                    if n >= 2:
                        pe.wait_ge(pt_copied, at + n - 1)
                    for j in range(units[n][0] + 1):
                        m = pe.transpose(bank[2 + n % 2][:, P * j:P * j + P], prob[:, n % 3, P * j:P * j + P], ident[:, :])
                    m.then_inc(pt_done, 1)

                def values(n):
                    pe.wait_ge(pt_copied, at + n + 1)
                    if n >= 2:
                        pe.wait_ge(o_done, at + n - 1)
                    last = units[n][0]
                    for j in range(last + 1):
                        m = pe.matmul(bank[4 + n % 2][:, 0:HD], probT[:, n % 2, P * j:P * j + P], v_of(run, units[n], j),
                                      start=(j == 0), stop=(j == last))
                    m.then_inc(pv_done, 1)

                def turn_out(m, i, r):
                    pe.wait_ge(o_done, at + done_for(m))
                    if OT_AT[run] + m:
                        pe.wait_ge(ot_lo, OT_AT[run] + m)
                    wide = OT_WIDE[run]
                    for f in range(wide):
                        tr = pe.transpose(turned(run)[:, P * f:P * f + P], block_out(run, i, wide * r + f), ident[:, :])
                    tr.then_inc(ot_done, 1)

                for n in range(3):
                    scores(n)
                for n in range(len(units)):
                    turn(n)
                    if n + 3 < len(units):
                        scores(n + 3)
                    if n >= 2:
                        values(n - 2)
                    for m, i, r in rounds_at(n):
                        turn_out(m, i, r)
                values(len(units) - 2)
                values(len(units) - 1)
                for m, i, r in rounds_at(len(units)):
                    turn_out(m, i, r)

            def gate_products(n):
                pe.wait_ge(small_landed, 16)
                for j in range(QB):
                    for k in range(KB):
                        for part in (h_hi, h_lo):
                            m = pe.matmul(bank[6][:, 32 * j:32 * j + n], part[:, k, P * j:P * j + P].bitcast(F32),
                                          w_small[:, k, 0:n], start=(k == 0 and part is h_hi),
                                          stop=(k == KB - 1 and part is h_lo))
                m.then_inc(gate_done, 1)

            pe.wait_ge(csil_ready, 1)
            pe.wait_ge(filled, 1)
            rstd(0)
            for q in range(MOD_FIRST):
                if q in ALONE:
                    first_mod_alone(q)
                else:
                    mod_panel(summed(q) % SUMS, summed(q), mod_column(q))

            def lru_gates(c):
                pe.wait_ge(conv_ready, c + 1)
                pe.wait_ge(lru_landed, 16)
                if c:
                    pe.wait_ge(lsig_ready, 2 * c)
                for w in range(2):
                    m = pe.matmul(bank[4 + w][:, :], lruw[:, w, c, :], xc[:, c, :], start=True, stop=True)
                m.then_inc(lgate_done, 1)

            def hidden(kv):
                pe.wait_ge(w1_landed, 16 * (3 + kv))
                pe.wait_ge(blocks_ready, kv + 1)
                pe.wait_ge(lsig_ready, 2 * LC)
                for l in range(CMP_LEN):
                    m = pe.matmul(bank[4 + kv][:, 0:64], w1[:, l, :], blocks[:, kv, l, :],
                                  start=(l == 0), stop=(l == CMP_LEN - 1))
                m.then_inc(hid_done, 1)

            for p in range(P_VS):
                panel(p, p % RING, h_hi, h_lo, moving=(h_lo_ready, 0) if p == 0 else None)
                with_mods(p)
                if 5 <= p < 5 + LC:
                    lru_gates(p - 5)
            hidden(0)
            token_panels(P_VS)
            with_mods(P_VS)
            with_mods(P_VW)
            pe.wait_ge(bank_free, P_OUT0)
            pe.wait_ge(hid_ready, 1)
            for gr in range(2):
                m = pe.matmul(bank[0][HD * gr:HD * gr + HD, 32 * gr:32 * gr + 32], w2[:, 0, :],
                              hid[:, 0, 32 * gr:32 * gr + 32], start=True, stop=True)
            m.then_inc(cmp_done, 1)
            hidden(1)
            pe.wait_ge(cmp_ready, 1)
            for i in range(QB):
                for c in range(4):
                    at = 256 * (i % 2) + 64 * c
                    m = pe.matmul(bank[2 + i // 2][:, at:at + 64], q0[:, c, P * i:P * i + P], kdiag[:, :],
                                  start=True, stop=True)
            m.then_inc(cs_done, 1)
            gate_products(3 * 8)
            pe.wait_ge(hid_ready, 2)
            for r in range(4):
                m = pe.matmul(bank[1][32 * r:32 * r + 32, HD * r:HD * r + HD], hid[:, 1, 32 * (r % 2):32 * (r % 2) + 32],
                              w2[:, 1, :], start=True, stop=True)
            m.then_inc(cmp_done, 1)
            pe.wait_ge(cexp_ready, 1)
            pe.wait_ge(cmp_ready, 2)
            for half in range(2):
                for i in range(QB):
                    m = pe.transpose(bank[half][:, P * i:P * i + P],
                                     cprob[:, i, 4 * half:4 * half + 4, :].rearrange("p h n -> p (h n)"), ident[:, :])
            m.then_inc(cpt_done, 1)
            pe.wait_ge(cpt_copied, 2)
            for i in range(QB):
                for half in range(2):
                    m = pe.matmul(bank[2 + i][:, 256 * half:256 * half + 256], cpT[:, half, i, :],
                                  vdiag[:, :, :].rearrange("p h d -> p (h d)"), start=True, stop=True)
                m.then_inc(cpv_done, 1)
            pe.wait_ge(co_done, QB)
            pe.wait_ge(keys_padded, 1)
            attention(0)
            for p in range(P_OUT0, P_OUT0 + KB):
                if p == P_OUT0:
                    pe.wait_ge(y_lo, LC)
                    pe.wait_ge(ot_lo, OT_AT[1])
                panel(p, p % RING, h_hi, h_lo)
                with_mods(p)
            rstd(1)
            ffn(0, P_FFN0, 1)
            rstd(2)

            for p in range(P_QI, P_V1):
                panel(p, p % RING, h_hi, h_lo, moving=(h_lo_ready, KB * H_OF[2]) if p == P_QI else None)
            token_panels(P_V1)
            panel(P_KI, P_KI % RING, h_hi, h_lo)
            pe.wait_ge(bank_free, P_Q1)
            n = 0
            for i in range(1, QB):
                for hh in range(IDX_HEADS):
                    if n >= 2:
                        pe.wait_ge(relu_ready, n - 1)
                    rows_ = slice(HD * (hh % 2), HD * (hh % 2) + HD)
                    pe.matmul(bank[4 + n % 2][:, 0:P * (i + 1)], qi[rows_, hh // 2, P * i:P * i + P],
                              kiT[rows_, 0:P * (i + 1)], start=True, stop=True).then_inc(idx_done, 1)
                    n += 1
            panels(P_Q1, KB + 1, h_hi, h_lo)
            pe.wait_ge(bank_free, P_OUT1)
            attention(1)
            pe.wait_ge(ot_lo, OT_AT[2])
            panels(P_OUT1, KB, h_hi, h_lo)
            rstd(3)
            ffn(1, P_FFN1, 3)
            rstd(4)

            rstd(5)
            panels(P_AG, 12, h_hi, h_lo, moving=(h_lo_ready, KB * H_OF[5]))
            for p in range(P_V2, P_OUT2, 2):
                token_panels(p)
            pe.wait_ge(vln_ready, 1)
            pe.wait_ge(ws_masked, 1)
            for c in range(4):
                if c >= 2:
                    pe.wait_ge(bias_added, c - 1)
                for j in range(QB):
                    for b in range(2):
                        at = HD * (2 * c + b)
                        m = pe.matmul(bank[4 + c % 2][HD * b:HD * b + HD, P * j:P * j + P], v2t[:, j, at:at + HD],
                                      wsT[:, 2 * c + b, :], start=True, stop=True)
                m.then_inc(mix_done, 1)
            pe.wait_ge(mean_acc, 1)
            pe.matmul(bank[6][:, :], ones[:, :], acc[:, :], start=True, stop=True).then_inc(mean_done, 1)
            pe.wait_ge(bias_added, 4)
            rstd(6)
            pe.wait_ge(y_lo, LC + KB)
            panels(P_OUT2, KB, h_hi, h_lo)
            rstd(7)
            ffn(2, P_FFN2, 7)
            rstd(8)

            def swapped(n):
                pe.wait_ge(rot_copied, n + 1)
                if n >= 2:
                    pe.wait_ge(rot_done, n - 1)
                pe.matmul(bank[4 + n % 2][:, :], swap[:, :], rot[:, n % 2, :], start=True, stop=True).then_inc(swap_done, 1)

            for p in range(P_Q3, P_V3):
                panel(p, p % RING, h_hi, h_lo, moving=(h_lo_ready, KB * H_OF[8]) if p == P_Q3 else None)
                if p > P_Q3:
                    swapped(p - P_Q3 - 1)
            token_panels(P_V3)
            swapped(2 * KB - 1)
            for p in range(P_V3 + 2, P_OUT3, 2):
                token_panels(p)
            pe.wait_ge(bank_free, P_OUT3)
            pe.wait_ge(rot_done, 2 * KB)
            attention(2)
            pe.wait_ge(ot_lo, OT_AT[2] + ROUNDS * QB)
            panels(P_OUT3, KB, h_hi, h_lo)
            rstd(9)
            ffn(3, P_FFN3, 9)
            rstd(10)

        @block.scalar
        def _(act):
            def split_hi(p, slot=None, landed=None):
                if isinstance(p, int):
                    if p >= N_PANELS:
                        return
                    slot, landed = p % RING, 16 * (p // RING + 1)
                act.wait_ge(raw_landed[slot], landed)
                if not isinstance(p, int) or p >= RING:
                    act.wait_ge(panel_done, p - RING + 1)
                act.activation(w_hi[:, slot, :], raw[:, slot, :], ACT.Copy).then_inc(hi_ready, 1)

            def split_hi_loop(it, p):
                split_hi(it * 4 + p, p % RING, it * 16 + 16 * (p // RING + 1))

            def square(r, n, src):
                if n >= 2:
                    act.wait_ge(squares_added, SQ_AT[r] + n - 1)
                act.activation(sq[:, n % 2, :], src, ACT.Square).then_inc(squares_ready, 1)

            def take_root(r, width=D):
                act.wait_ge(sums_ready, r + 1)
                act.activation(root[:, 0:QB], bank[4][:, 0:QB], ACT.Sqrt, bias=EPS, scale=1.0 / width)\
                    .then_inc(root_ready, 1)

            def h_high(r):
                for k in range(KB):
                    act.wait_ge(t_ready, KB * H_OF[r] + k + 1)
                    act.activation(h_hi[:, k, :], tn[:, k % 2, :], ACT.Identity, bias=shift(r, k)).then_inc(h_hi_ready, 1)

            def project(p0, r):
                for n in range(KB):
                    split_hi(p0 + n + RING)
                    act.wait_ge(bank_free, p0 + n + 1)
                    square(r, n, x[:, n, :])

            def ffn(layer, p0, r):
                f, p = FC * layer, p0
                for part, size in enumerate(PARTS):
                    with act.Fori(0, size // 2) as it:
                        for a in range(2):
                            slot = (p + 2 * a) % RING
                            if layer < 2:
                                act.wait_ge(panel_done, it * 4 + (p + 2 * a + 1))
                                act.activation(silu[:, a, :], bank[slot][:, :], ACT.Silu).then_inc(silu_ready, 1)
                                split_hi_loop(it, p + 2 * a + RING)
                            else:
                                split_hi_loop(it, p + 2 * a + RING)
                                act.wait_ge(cgate_ready, it * 2 + (f + a + 1 - 2 * FC))
                                act.activation(silu[:, a, :], cgate[:, a, :], ACT.Silu).then_inc(silu_ready, 1)
                            act.wait_ge(prod_ready, it * 2 + (f + a + 1))
                            act.activation(g_hi[:, it * 2 + a, :], prod[:, a, :], ACT.Copy).then_inc(f_hi_ready, 1)
                            split_hi_loop(it, p + 2 * a + 1 + RING)
                    p += 2 * size
                    f += size
                    if part < len(PARTS) - 1:
                        with act.Fori(0, KB // 4) as it:
                            for j in range(4):
                                split_hi_loop(it, p + j + RING)
                    else:
                        project(p, r + 1)
                    p += KB

            def attention(run):
                units, at = (UNITS0, UNITS1, UNITS1)[run], U_AT[run]

                def copy_turned(n):
                    act.wait_ge(pt_done, at + n + 1)
                    if n >= 2:
                        act.wait_ge(pv_done, at + n - 1)
                    w = P * (units[n][0] + 1)
                    act.activation(probT[:, n % 2, 0:w], bank[2 + n % 2][:, 0:w], ACT.Copy).then_inc(pt_copied, 1)

                def out_high(m, i, r):
                    wide = OT_WIDE[run]
                    f = FIRST_OUT[run] + wide * r
                    act.wait_ge(ot_done, OT_AT[run] + m + 1)
                    act.activation(h_hi[:, f:f + wide, P * i:P * i + P],
                                   turned(run).rearrange("p (f t) -> p f t", f=wide), ACT.Copy).then_inc(ot_hi, 1)

                for n, unit in enumerate(units):
                    u, w = at + n, P * (unit[0] + 1)
                    act.wait_ge(masked_ready, u + 1)
                    if n >= 3:
                        act.wait_ge(pt_done, u - 2)
                    act.activation(prob[:, n % 3, 0:w], srow[:, n % 2, 0:w], ACT.Exp, bias=stat[:, 0, u % 64:u % 64 + 1],
                                   scale=SCALE, accum_out=stat[:, 1, u % 64:u % 64 + 1]).then_inc(exp_ready, 1)
                    if n:
                        copy_turned(n - 1)
                    for m, i, r in rounds_at(n - 1):
                        out_high(m, i, r)
                copy_turned(len(units) - 1)
                for m, i, r in rounds_at(len(units)):
                    out_high(m, i, r)

            act.dma_start(ident[:, :], A["ident"]).then_inc(consts_landed, 16)
            act.dma_start(swap[:, :], A["swap"]).then_inc(consts_landed, 16)

            act.wait_ge(consts_landed, 48)
            act.activation(csil[:, :], cols[:, COLS["c"]:COLS["c"] + KB], ACT.Silu).then_inc(csil_ready, 1)
            act.wait_ge(filled, 2)
            act.activation(sp[:, 1, :], sp[:, 0, :], ACT.Exp, scale=-1.0).then_inc(spexp, 1)
            act.wait_ge(x_landed, 16)
            for n in range(KB):
                square(0, n, x[:, n, :])
            take_root(0)
            act.wait_ge(mod_used, MOD_FIRST // 2)
            act.dma_start(mask[:, :, :], A["causal"]).then_inc(masks_landed, 16)
            act.dma_start(cmask[:, :, :], A["cmask"]).then_inc(masks_landed, 16)
            act.dma_start(w_small[:, :, 0:24], A["w_gates"]).then_inc(small_landed, 16)
            act.dma_start(w1[:, :, :], A["w1"][0]).then_inc(w1_landed, 16)
            act.dma_start(w2[:, :, :], A["w2"]).then_inc(w1_landed, 16)
            act.dma_start(peT[:, :, :], A["pe"]).then_inc(w1_landed, 16)
            for p in range(RING):
                split_hi(p)
            h_high(0)
            act.wait_ge(squares_added, KB)
            act.dma_start(lruw[:, :, :, :], A["lruw"]).then_inc(lru_landed, 16)

            for p in range(P_OUT0):
                if 6 <= p < 6 + LC:
                    c = p - 6
                    act.wait_ge(lgate_done, c + 1)
                    act.activation(rt[:, c, 0:T], bank[4][:, :], ACT.Sigmoid, bias=col("ba", c)).then_inc(lsig_ready, 1)
                    act.activation(inp[:, c, :], bank[5][:, :], ACT.Sigmoid, bias=col("bx", c)).then_inc(lsig_ready, 1)
                if p == 10:
                    act.wait_ge(bank_free, P_AGATE + LC)
                    for c in range(LC):
                        act.activation(ya[:, c, :], ya[:, c, :], ACT.Gelu_apprx_tanh).then_inc(agelu_ready, 1)
                if 11 <= p < 11 + LC:
                    c = p - 11
                    t = rt[:, c, 0:T]
                    act.wait_ge(lsig_ready, 2 * c + 2)
                    if c >= 2:
                        act.wait_ge(y_ready, c - 1)
                    act.activation(decay[:, c % 2, :], t, ACT.Exp, scale=sp[:, 2, c:c + 1]).then_inc(ldecay_ready, 1)
                    act.wait_ge(ldecay_ready, c + 1)
                    act.activation(t, t, ACT.Tanh, scale=sp[:, 5, c:c + 1]).then_inc(ltanh_ready, 1)
                    act.wait_ge(ltanh_ready, c + 1)
                    act.activation(t, t, ACT.Sqrt).then_inc(lsqrt_ready, 1)
                if p == P_VS:
                    act.wait_ge(hid_done, 1)
                    act.dma_start(w1[:, :, :], A["w1"][1]).then_inc(w1_landed, 16)
                    act.activation(hid[:, 0, :], bank[4][:, 0:64], ACT.Gelu_apprx_tanh).then_inc(hid_ready, 1)
                split_hi(p + RING)
            act.wait_ge(hid_done, 2)
            act.activation(hid[:, 1, :], bank[5][:, 0:64], ACT.Gelu_apprx_tanh).then_inc(hid_ready, 1)
            act.wait_ge(gate_done, 1)
            act.activation(small[:, :, :], bank[6][:, 0:P].rearrange("p (j n) -> p j n", n=32)[:, :, 0:24], ACT.Sigmoid)\
                .then_inc(gate_ready, 1)
            act.wait_ge(cmax_ready, 1)
            act.activation(cprob[:, :, :, :], cprob[:, :, :, :], ACT.Exp, scale=SCALE).then_inc(cexp_ready, 1)
            for c in range(LC):
                act.wait_ge(y_ready, c + 1)
                act.activation(h_hi[:, c, :], ya[:, c, :], ACT.Copy).then_inc(y_hi, 1)
            act.wait_ge(cpt_done, 1)
            for half in range(2):
                act.activation(cpT[:, half, :, :], bank[half][:, :].rearrange("p (i t) -> p i t", i=QB), ACT.Copy)\
                    .then_inc(cpt_copied, 1)
            attention(0)
            project(P_OUT0, 1)
            take_root(1)
            h_high(1)
            ffn(0, P_FFN0, 1)
            take_root(2)
            h_high(2)

            for p in range(P_QI, P_Q1):
                split_hi(p + RING)
            for n in range((QB - 1) * IDX_HEADS):
                w = P * (n // IDX_HEADS + 2)
                act.wait_ge(idx_done, n + 1)
                if n >= 2:
                    act.wait_ge(idx_added, n - 1)
                act.activation(irel[:, n % 2, 0:w], bank[4 + n % 2][:, 0:w], ACT.Relu, scale=IDX_SCALE).then_inc(relu_ready, 1)
            for p in range(P_Q1, P_OUT1):
                split_hi(p + RING)
            attention(1)
            act.dma_start(mask[:, :, :], A["dilated"]).then_inc(masks_landed, 16)
            act.dma_start(wsT[:, :, :], A["wsT"]).then_inc(layer2_landed, 16)
            act.dma_start(rows[:, :, :], A["rows"]).then_inc(layer2_landed, 16)
            act.dma_start(bs[:, :, :], A["bs"]).then_inc(layer2_landed, 16)
            project(P_OUT1, 3)
            take_root(3)
            h_high(3)
            ffn(1, P_FFN1, 3)
            take_root(4)
            for n in range(KB):
                act.wait_ge(x_norm, n + 1)
                square(5, n, x[:, n, :])
            take_root(5)
            h_high(5)

            for c in range(4):
                split_hi(P_AG + 2 * c + RING)
                p = P_AG + 2 * c + 1
                act.wait_ge(panel_done, p + 1)
                if c >= 2:
                    act.wait_ge(bank_free, p - 3)
                act.activation(sg[:, c % 2, :], bank[p % RING][:, :], ACT.Sigmoid, bias=col("bgg", c)).then_inc(sg_ready, 1)
                split_hi(p + RING)
            act.wait_ge(pad_ready, 1)
            for p in range(P_U, P_OUT2):
                split_hi(p + RING)
                for k in taps_beside(p):
                    if k > 2:
                        act.wait_ge(tap_added, k - 2)
                    act.activation(tapped[:, k % 2, :], pad[:, 3, k:k + T], ACT.Copy, scale=col("cconv", 4 * k + 3))\
                        .then_inc(tap_made, 1)
            for c in range(4):
                act.wait_ge(bank_free, P_U + c + 1)
                act.activation(u2[:, c, :], u2[:, c, :], ACT.Gelu_apprx_tanh).then_inc(u_ready, 1)
            act.wait_ge(bank_free, P_V2 + 4)
            act.activation(v2t[:, :, :], v2t[:, :, :], ACT.Gelu_apprx_tanh).then_inc(v_gelu, 1)
            act.wait_ge(var_ready, 1)
            act.activation(lnst[:, :, 8:9], lnst[:, :, 7:8], ACT.Sqrt, bias=EPS).then_inc(vstd_ready, 1)
            for c in range(4):
                act.wait_ge(y_ready, LC + c + 1)
                act.activation(h_hi[:, c, :], ysp[:, c % 2, :], ACT.Copy).then_inc(y_hi, 1)
            for c in range(4):
                act.wait_ge(centred, c + 1)
                square(6, c, cout[:, c, :])
            take_root(6, 512)
            for c in range(4):
                act.wait_ge(cn_ready, c + 1)
                act.activation(ysp[:, c % 2, :], ysp[:, c % 2, :], ACT.Silu, bias=col("clnb", c)).then_inc(csilu_ready, 1)
                act.wait_ge(csilu_ready, c + 1)
                act.activation(h_hi[:, 4 + c, :], ysp[:, c % 2, :], ACT.Copy).then_inc(y_hi, 1)
            project(P_OUT2, 7)
            act.dma_start(rope[:, :, :], A["rope"]).then_inc(rope_landed, 16)
            take_root(7)
            h_high(7)
            ffn(2, P_FFN2, 7)
            take_root(8)
            h_high(8)

            for p in range(P_Q3, P_V3):
                n = p - P_Q3
                act.wait_ge(panel_done, p + 1)
                if n >= 2:
                    act.wait_ge(swap_done, n - 1)
                act.activation(rot[:, n % 2, :], bank[p % RING][:, :], ACT.Copy).then_inc(rot_copied, 1)
                split_hi(p + RING)
            for p in range(P_V3, P_OUT3):
                split_hi(p + RING)
            attention(2)
            project(P_OUT3, 9)
            take_root(9)
            h_high(9)
            ffn(3, P_FFN3, 9)
            take_root(10)
            for k in range(KB):
                act.wait_ge(yout_ready, k + 1)
                act.dma_start(A["out"][k], yout[:, k, :]).then_inc(yout_stored, 16)
            act.wait_ge(yout_stored, 16 * KB)

        @block.vector
        def _(dve):
            MUL, ADD, SUB = ALU.mult, ALU.add, ALU.subtract

            def panel_ready(p):
                dve.wait_ge(panel_done, p + 1)

            def copy_out(p, out):
                panel_ready(p)
                dve.tensor_copy(out, bank[p % RING][:, :]).then_inc(bank_free, 1)

            def tokens_of(p, half):
                return bank[p % RING + half][:, :].rearrange("p (j n) -> p j n", j=2)

            def copy_tokens(p, out, at):
                panel_ready(p + 1)
                for half in range(2):
                    dve.tensor_copy(out[:, 2 * half:2 * half + 2, at:at + 2 * P], tokens_of(p, half)).then_inc(bank_free, 1)

            def add_square(r, n):
                dve.wait_ge(squares_ready, SQ_AT[r] + n + 1)
                if n == 0:
                    dve.tensor_copy(acc[:, :], sq[:, 0, :]).then_inc(squares_added, 1)
                else:
                    dve.drain()
                    dve.tensor_tensor(acc[:, :], acc[:, :], sq[:, n % 2, :], ADD).then_inc(squares_added, 1)

            def rstd(r):
                dve.drain()
                dve.sem_inc(acc_ready, 1)
                dve.wait_ge(root_ready, r + 1)
                dve.reciprocal(root[:, QB:2 * QB], root[:, 0:QB])
                dve.drain()
                for j in range(QB):
                    m = dve.tensor_scalar(diag[:, j, :], ident[:, :], root[:, QB + j:QB + j + 1], None, MUL)
                m.then_inc(diag_ready, 1)
                dve.wait_ge(rstd_ready, r + 1)

            def norm_h(r, after_rstd=None):
                rstd(r)
                if after_rstd is not None:
                    after_rstd()
                at = KB * H_OF[r]

                def low(k):
                    dve.wait_ge(h_hi_ready, at + k + 1)
                    dve.scalar_tensor_tensor(out=h_lo[:, k, :], in0=tn[:, k % 2, :], scalar=shift(r, k),
                                             in1=h_hi[:, k, :].bitcast(F32), op0=ADD, op1=SUB).then_inc(h_lo_ready, 1)

                for k in range(KB):
                    dve.drain()
                    dve.scalar_tensor_tensor(out=tn[:, k % 2, :], in0=x[:, k, :], scalar=gain(r, k), in1=bank[5][:, :],
                                             op0=MUL, op1=MUL).then_inc(t_ready, 1)
                    if k:
                        dve.drain()
                        low(k - 1)
                dve.drain()
                low(KB - 1)
                dve.drain()

            def add_x(p, n, scale_by):
                panel_ready(p)
                dve.scalar_tensor_tensor(out=x[:, n, :], in0=bank[p % RING][:, :], scalar=scale_by, in1=x[:, n, :],
                                         op0=MUL, op1=ADD).then_inc(bank_free, 1)

            def project(layer, p0, r, is_ffn=False):
                dve.drain()
                for n in range(KB):
                    sum_mods(p0 + n + AHEAD)
                    add_x(p0 + n, n, out_gate(layer, is_ffn, n))
                    if n:
                        add_square(r, n - 1)
                add_square(r, KB - 1)

            def conv3(layer, it, p, tap, out, n_col):
                name, slot = ("fw2", "fb2") if layer == 2 else ("fw3", "fb3"), p % RING
                dve.wait_ge(panel_done, it * 4 + (p + 1))

                def w(what, at):
                    a = COLS[what] + at
                    return cols[:, a:a + FC].rearrange("p (n o) -> p n o", o=1)[:, n_col, :]

                first = tap * FC
                dve.tensor_scalar(out, bank[slot][:, :], w(name[0], (TAPS_FFN - 1) * 2 * FC + first),
                                  w(name[1], first), MUL, ADD)
                for back in range(1, TAPS_FFN):
                    dve.drain()
                    m = dve.scalar_tensor_tensor(out=out[:, back:T], in0=bank[slot][:, 0:T - back],
                                                 scalar=w(name[0], (TAPS_FFN - 1 - back) * 2 * FC + first),
                                                 in1=out[:, back:T], op0=MUL, op1=ADD)
                return m

            def ffn(layer, p0, r):
                f, p = FC * layer, p0
                for part, size in enumerate(PARTS):
                    dve.drain()
                    with dve.Fori(0, size // 2) as it:
                        for a in range(2):
                            pg, pu = p + 2 * a, p + 2 * a + 1
                            if layer < 2:
                                dve.wait_ge(silu_ready, it * 2 + (f + a + 1))
                                dve.wait_ge(panel_done, it * 4 + (pu + 1))
                                dve.tensor_tensor(prod[:, a, :], silu[:, a, :], bank[pu % RING][:, :], MUL)\
                                    .then_inc(prod_ready, 1)
                                dve.drain()
                                dve.sem_inc(bank_free, 2)
                            else:
                                n_col = it * 2 + (f - FC * layer + a)
                                conv3(layer, it, pg, 0, cgate[:, a, :], n_col).then_inc(bank_free, 1)
                                dve.drain()
                                dve.sem_inc(cgate_ready, 1)
                                conv3(layer, it, pu, 1, cval[:, :], n_col).then_inc(bank_free, 1)
                                dve.drain()
                                dve.wait_ge(silu_ready, it * 2 + (f + a + 1))
                                dve.tensor_tensor(prod[:, a, :], silu[:, a, :], cval[:, :], MUL).then_inc(prod_ready, 1)
                                dve.drain()
                            dve.wait_ge(f_hi_ready, it * 2 + (f + a + 1))
                            dve.tensor_tensor(g_lo[:, it * 2 + a, :], prod[:, a, :], g_hi[:, it * 2 + a, :].bitcast(F32), SUB)\
                                .then_inc(f_lo_ready, 1)
                            if p < MOD_UNTIL:
                                sum_mod_loop(it, pg + AHEAD)
                                sum_mod_loop(it, pu + AHEAD)
                        dve.drain()
                    p += 2 * size
                    f += size
                    if part < len(PARTS) - 1:
                        for n in range(KB):
                            sum_mods(p + n + AHEAD)
                            add_x(p + n, n, out_gate(layer, True, n))
                    else:
                        project(layer, p, r + 1, True)
                    p += KB

            def attention(run, beside=None, times=0):
                units, at = (UNITS0, UNITS1, UNITS1)[run], U_AT[run]
                half = len(units) // 2 - 2
                assert times <= half

                def output(n):
                    u = at + n
                    i, c, b, br = units[n]
                    factor = stat[:, 2, u % 64:u % 64 + 1]
                    if run == 0:
                        g_at = 3 * head_of(0, units[n]) + br
                        dve.tensor_scalar(factor, factor, small[:, i, g_at:g_at + 1], None, MUL)
                        dve.drain()
                    dve.wait_ge(pv_done, u + 1)
                    o = o_of(run, units[n])
                    if run == 0:
                        dve.scalar_tensor_tensor(out=o, in0=bank[4 + n % 2][:, 0:HD], scalar=factor, in1=o,
                                                 op0=MUL, op1=ADD).then_inc(o_done, 1)
                    else:
                        dve.tensor_scalar(o, bank[4 + n % 2][:, 0:HD], factor, None, MUL).then_inc(o_done, 1)

                def invert(n):
                    u = (at + n) % 64
                    dve.wait_ge(exp_ready, at + n + 1)
                    dve.reciprocal(stat[:, 2, u:u + 1], stat[:, 1, u:u + 1])

                def out_low(m, i, r):
                    wide = OT_WIDE[run]
                    f = FIRST_OUT[run] + wide * r
                    dve.wait_ge(ot_hi, OT_AT[run] + m + 1)
                    dve.tensor_tensor(h_lo[:, f:f + wide, P * i:P * i + P],
                                      turned(run).rearrange("p (f t) -> p f t", f=wide),
                                      h_hi[:, f:f + wide, P * i:P * i + P].bitcast(F32), SUB).then_inc(ot_lo, 1)

                for n, unit in enumerate(units):
                    i = unit[0]
                    u, w = at + n, P * (i + 1)
                    if n >= 2:
                        invert(n - 2)
                    dve.wait_ge(score_ready, u + 1)
                    top = stat[:, 0, u % 64:u % 64 + 1]
                    dve.tensor_tensor_reduce(srow[:, n % 2, 0:w], bank[SBANK[n % 3]][:, 0:w], mask[:, i, 0:w], 1.0, LOWEST,
                                             ADD, ALU.max, top)
                    dve.drain()
                    dve.tensor_scalar(top, top, -SCALE, None, MUL).then_inc(masked_ready, 1)
                    if n >= 4:
                        output(n - 4)
                    if n < half and (n + 1) * times // half > n * times // half:
                        beside()
                    for m, ii, r in rounds_at(n - 2):
                        out_low(m, ii, r)
                for n in range(len(units) - 4, len(units)):
                    if n >= len(units) - 2:
                        invert(n)
                        dve.drain()
                    output(n)
                for m, ii, r in rounds_at(len(units)):
                    out_low(m, ii, r)
                dve.drain()

            def add_mods(a, b):
                dve.wait_ge(mod_used, b)
                at = COLS["modb"]
                dve.tensor_tensor(modv[:, a:b], MODBANK[:, a:b], cols[:, at + a:at + b], ADD)
                dve.drain()

            def set_gains(r):
                at = (r // 2) * MOD + (1 if r % 2 == 0 else 4) * KB
                own = COLS[("g0mix", "g0ffn", "g1mix", "g1ffn")[r]]
                dve.scalar_tensor_tensor(out=gains[:, KB * r:KB * r + KB], in0=modv[:, at:at + KB], scalar=1.0,
                                         in1=cols[:, own:own + KB], op0=ADD, op1=MUL)
                dve.drain()

            def sum_mod(panel_, landed, landed_value, used, sum_slot):
                dve.wait_ge(landed, landed_value)
                w = panel_.rearrange("p (k n) -> p k n", n=P)
                dve.tensor_tensor(w, w, csil[:, :].rearrange("p (k o) -> p k o", o=1).broadcast_to((P, KB, P)), MUL)
                dve.drain()
                if used is not None:
                    dve.wait_ge(mod_used, used)
                dve.tensor_reduce(modsum[:, sum_slot, :], panel_.rearrange("p (k n) -> p n k", n=P), AX_X, ADD)\
                    .then_inc(mod_summed, 1)

            def first_sums():
                dve.wait_ge(csil_ready, 1)
                by_dve = [q for q in range(MOD_FIRST) if q not in ALONE]
                for n, q in enumerate(by_dve):
                    sum_mod(first_mods[q // 4][:, q % 4, :], first_landed[q // 4], 16,
                            by_dve[n - SUMS] + 1 if n >= SUMS else None, summed(q) % SUMS)

            def sum_mods(p):
                for q in mods_beside(p):
                    sum_mod(modraw[:, q % MRING, :], mod_landed[q % MRING], 16 * ((q - MOD_FIRST) // MRING + 1),
                            q - SUMS + 1, summed(q) % SUMS)

            def sum_mod_loop(it, p):
                q = mods_beside(p)[0]
                sum_mod(modraw[:, q % MRING, :], mod_landed[q % MRING], it * 32 + 16 * ((q - MOD_FIRST) // MRING + 1),
                        it * 4 + (q - SUMS + 1), summed(q) % SUMS)

            dve.memset(ones[:, :], 1.0)
            dve.memset(plain[:, 0:1], 1.0)
            dve.memset(plain[:, 1:2], 0.0)
            dve.memset(own_half[:, :], 0.0)
            dve.drain()
            for b in range(2):
                dve.memset(own_half[HD * b:HD * b + HD, b:b + 1], 1.0)
            dve.drain()
            dve.sem_inc(filled, 1)
            lam = cols[:, COLS["lam"]:COLS["lam"] + LC]
            dve.wait_ge(consts_landed, 48)
            dve.tensor_scalar(sp[:, 2, :], lam, -1.0, None, MUL)
            dve.drain()
            dve.tensor_tensor(sp[:, 0, :], sp[:, 2, :], lam, ALU.max).then_inc(filled, 1)
            dve.wait_ge(spexp, 1)
            dve.tensor_scalar(sp[:, 2, :], sp[:, 1, :], 2.0, None, ADD)
            dve.drain()
            dve.reciprocal(sp[:, 3, :], sp[:, 2, :])
            dve.drain()
            dve.tensor_tensor(sp[:, 2, :], sp[:, 1, :], sp[:, 3, :], MUL)
            dve.drain()
            dve.tensor_tensor(sp[:, 3, :], sp[:, 2, :], sp[:, 2, :], MUL)
            dve.drain()
            dve.tensor_scalar(sp[:, 4, :], sp[:, 3, :], 1.0 / 17, None, MUL)
            for odd in (15, 13, 11, 9, 7, 5, 3):
                dve.drain()
                dve.scalar_tensor_tensor(out=sp[:, 4, :], in0=sp[:, 4, :], scalar=1.0 / odd, in1=sp[:, 3, :],
                                         op0=ADD, op1=MUL)
            dve.drain()
            dve.scalar_tensor_tensor(out=sp[:, 4, :], in0=sp[:, 4, :], scalar=1.0, in1=sp[:, 2, :], op0=ADD, op1=MUL)
            dve.tensor_scalar(sp[:, 3, :], lam, -1.0, 0.0, MUL, ALU.max)
            dve.drain()
            dve.scalar_tensor_tensor(out=sp[:, 5, :], in0=sp[:, 4, :], scalar=2.0, in1=sp[:, 3, :], op0=MUL, op1=ADD)
            dve.drain()
            dve.tensor_scalar(sp[:, 5, :], sp[:, 5, :], LRU_C / 2, None, MUL)
            dve.drain()
            dve.tensor_scalar(sp[:, 2, :], sp[:, 5, :], -2.0, None, MUL)
            dve.drain()

            for n in range(KB):
                add_square(0, n)

            def first_gains():
                first_sums()
                add_mods(0, MOD_FIRST)
                dve.memset(axp[:, :, 0:TAPS_LRU - 1], 0.0)
                set_gains(0)

            norm_h(0, first_gains)

            def lru_conv(c):
                dve.drain()
                dve.tensor_scalar(xc[:, c, :], axp[:, c, 0:T], col("lconv", c), col("lconvb", c), MUL, ADD)
                for k in range(1, TAPS_LRU):
                    dve.drain()
                    m = dve.scalar_tensor_tensor(out=xc[:, c, :], in0=axp[:, c, k:k + T], scalar=col("lconv", LC * k + c),
                                                 in1=xc[:, c, :], op0=MUL, op1=ADD)
                m.then_inc(conv_ready, 1)

            def lru_scan(c):
                t, a = rt[:, c, 0:T], decay[:, c % 2, :]
                dve.drain()
                dve.tensor_tensor(inp[:, c, :], inp[:, c, :], xc[:, c, :], MUL)
                dve.wait_ge(ldecay_ready, c + 1)
                dve.wait_ge(lsqrt_ready, c + 1)
                dve.memset(rt[:, c, 0:1], 1.0)
                dve.drain()
                dve.tensor_tensor(inp[:, c, :], inp[:, c, :], t, MUL)
                dve.drain()
                dve.scalar_tensor_tensor(out=inp[:, c, 1:T], in0=a[:, 1:T], scalar=1.0, in1=inp[:, c, 1:T],
                                         op0=ADD, op1=MUL)
                dve.drain()
                dve.tensor_tensor_scan(xc[:, c, :], a, inp[:, c, :], 0.0, MUL, ADD)
                dve.wait_ge(agelu_ready, c + 1)
                dve.drain()
                dve.tensor_tensor(ya[:, c, :], ya[:, c, :], xc[:, c, :], MUL).then_inc(y_ready, 1)

            def lay_blocks(kv, src):
                dve.memset(blocks[:, kv, :, :], 0.0)
                dve.drain()
                for gr in range(2):
                    rows_ = slice(HD * gr, HD * gr + HD)
                    runs = src[rows_, :].rearrange("p (n l) -> p l n", l=CMP_STRIDE)
                    for run in range(2):
                        ls = slice(CMP_STRIDE * run, CMP_STRIDE * run + CMP_STRIDE)
                        pos = peT[rows_, kv, ls].rearrange("p (l o) -> p l o", o=1)
                        m = dve.tensor_tensor(blocks[rows_, kv, ls, 32 * gr:32 * gr + NCMP], runs[:, :, run:run + NCMP],
                                              pos.broadcast_to((HD, CMP_STRIDE, NCMP)), ADD)
                dve.drain()
                dve.sem_inc(blocks_ready, 1)

            for p in range(AHEAD):
                sum_mods(p)
            for p in range(P_OUT0):
                sum_mods(p + AHEAD)
                if p < P_AGATE:
                    copy_out(p, axp[:, p, TAPS_LRU - 1:])
                elif p < P_Q0:
                    copy_out(p, ya[:, p - P_AGATE, :])
                    lru_conv(p - P_AGATE)
                elif p < P_KC:
                    copy_out(p, q0[:, p - P_Q0, :])
                elif p < P_VS:
                    copy_out(p, {P_KC: kcT, P_VC: vcT, P_KS: ksT, P_KW: kwT}[p][:, :])
                elif p == P_VW:
                    copy_tokens(P_VS, vtok0, 0)
                if 11 <= p < 11 + LC:
                    lru_scan(p - 11)
                if p == P_VS - 1:
                    dve.wait_ge(w1_landed, 48)
                    dve.drain()
                    lay_blocks(0, kcT)
                    lay_blocks(1, vcT)
                    dve.memset(kdiag[:, :], 0.0)
                    dve.drain()
            dve.wait_ge(cmp_done, 1)
            for gr in range(2):
                rows_ = slice(HD * gr, HD * gr + HD)
                dve.tensor_copy(kdiag[rows_, 32 * gr:32 * gr + 32], bank[0][rows_, 32 * gr:32 * gr + 32])
            dve.drain()
            dve.sem_inc(cmp_ready, 1)
            top, total, factor, gated = (cst[:, w, :, :] for w in range(4))

            def per_head(column):
                return column.rearrange("p i h -> p (i h)").rearrange("p (h o) -> p h o", o=1).broadcast_to((P, QB * 8, 32))

            heads = cprob[:, :, :, :].rearrange("p i h n -> p (i h) n")
            dve.wait_ge(masks_landed, 32)
            dve.wait_ge(cs_done, 1)
            for i in range(QB):
                dve.tensor_tensor(cprob[:, i, :, :],
                                  bank[2 + i // 2][:, 256 * (i % 2):256 * (i % 2) + 256].rearrange("p (h n) -> p h n", n=32),
                                  cmask[:, i:i + 1, :].broadcast_to((P, 8, 32)), ADD)
            dve.drain()
            dve.tensor_reduce(top.rearrange("p i h -> p (i h)"), heads, AX_X, ALU.max)
            dve.drain()
            dve.tensor_scalar(top, top, NEG / 1e10, None, ALU.max)
            dve.drain()
            dve.tensor_tensor(heads, heads, per_head(top), SUB).then_inc(cmax_ready, 1)
            dve.memset(vdiag[:, :, :], 0.0)
            dve.drain()
            dve.wait_ge(cmp_done, 2)
            for r in range(4):
                rows_ = slice(32 * r, 32 * r + 32)
                dve.tensor_copy(vdiag[rows_, r, :], bank[1][rows_, HD * r:HD * r + HD])
            dve.drain()
            dve.sem_inc(cmp_ready, 1)
            dve.wait_ge(cexp_ready, 1)
            dve.tensor_reduce(total.rearrange("p i h -> p (i h)"), heads, AX_X, ADD)
            dve.drain()
            dve.tensor_scalar(total, total, 1e-30, None, ALU.max)
            dve.drain()
            dve.reciprocal(factor, total)
            dve.drain()
            dve.wait_ge(gate_ready, 1)
            for i in range(QB):
                gates = small[:, i, :].rearrange("p (b c n) -> p c b n", b=2, n=3)[:, :, :, 0]
                dve.tensor_tensor(gated[:, i, :].rearrange("p (c b) -> p c b", b=2),
                                  factor[:, i, :].rearrange("p (c b) -> p c b", b=2), gates, MUL)
            dve.drain()
            for c in range(LC):
                dve.wait_ge(y_hi, c + 1)
                dve.tensor_tensor(h_lo[:, c, :], ya[:, c, :], h_hi[:, c, :].bitcast(F32), SUB).then_inc(y_lo, 1)
            for i in range(QB):
                dve.wait_ge(cpv_done, i + 1)
                dve.tensor_tensor(orow[:, i, :].rearrange("p (b c d) -> p c b d", b=2, d=HD),
                                  bank[2 + i][:, :].rearrange("p (c b d) -> p c b d", b=2, d=HD),
                                  gated[:, i, :].rearrange("p (c b o) -> p c b o", b=2, o=1).broadcast_to((P, 4, 2, HD)),
                                  MUL).then_inc(co_done, 1)
            add_mods(MOD_FIRST, MOD - KB)
            attention(0)
            project(0, P_OUT0, 1)
            add_mods(MOD - KB, MOD)
            set_gains(1)
            norm_h(1)
            ffn(0, P_FFN0, 1)
            add_mods(MOD, 2 * MOD)
            set_gains(2)
            set_gains(3)
            norm_h(2)

            for p in range(P_QI, P_V1):
                copy_out(p, qi[:, p - P_QI, :])
            panel_ready(P_V1 + 1)
            for half in range(2):
                both = tokens_of(P_V1, half)
                dve.tensor_copy(small[:, 2 * half:2 * half + 2, 0:IDX_HEADS], both[:, :, P:P + IDX_HEADS])
                dve.tensor_copy(v1t[:, 2 * half:2 * half + 2, :], both[:, :, 0:P]).then_inc(bank_free, 1)
            copy_out(P_KI, kiT[:, :])
            dve.drain()
            for n in range((QB - 1) * IDX_HEADS):
                i, hh = n // IDX_HEADS + 1, n % IDX_HEADS
                w = P * (i + 1)
                score = iacc[:, i - 1, 0:w]
                dve.wait_ge(relu_ready, n + 1)
                dve.drain()
                dve.scalar_tensor_tensor(out=score, in0=irel[:, n % 2, 0:w], scalar=small[:, i, hh:hh + 1],
                                         in1=mask[:, i, 0:w] if hh == 0 else score, op0=MUL, op1=ADD)\
                    .then_inc(idx_added, 1)
            dve.drain()
            picks = [(i, n) for i in reversed(range(1, QB)) for n in range(TOPK // 8)]

            def pick():
                i, n = picks.pop(0)
                score, best = iacc[:, i - 1, 0:P * (i + 1)], top8[:, n % 3, :]
                dve.max(best, score)
                dve.drain()
                dve.match_replace(out=score, in_to_replace=best, in_values=score, imm_value=TAKEN)
                dve.drain()
                if n == TOPK // 8 - 1:
                    dve.tensor_scalar(mask[:, i, 0:P * (i + 1)], score, TAKEN / 1.5, NEG, ALU.is_gt, MUL)

            dve.memset(k1pad[HD:P, 0, :], 0.0)
            dve.memset(k1pad[0:HD, 1, :], 0.0)
            for p in range(P_Q1, P_OUT1):
                if p < P_K1:
                    copy_out(p, q1[:, p - P_Q1, :])
                else:
                    panel_ready(p)
                    for b in range(2):
                        m = dve.tensor_copy(k1pad[HD * b:HD * b + HD, b, :], bank[p % RING][HD * b:HD * b + HD, :])
                    dve.drain()
                    dve.sem_inc(bank_free, 1)
                for _n in range(3):
                    if picks:
                        pick()
            while picks and picks[0][0] == QB - 1:
                pick()
            dve.drain()
            attention(1, pick if picks else None, len(picks))
            project(1, P_OUT1, 3)
            norm_h(3)
            ffn(1, P_FFN1, 3)
            rstd(4)
            for k in range(KB):
                dve.scalar_tensor_tensor(out=x[:, k, :], in0=x[:, k, :], scalar=gain(4, k), in1=bank[5][:, :],
                                         op0=MUL, op1=MUL).then_inc(x_norm, 1)
            for k in range(KB):
                add_square(5, k)
            norm_h(5)

            dve.memset(pad[:, :, 0:TAPS_CONV - 1], 0.0)
            dve.wait_ge(layer2_landed, 48)
            left = {c: list(range(DVE_TAPS3 if c == 3 else 0, TAPS_CONV)) for c in range(4)}
            undrained = set()

            def conv_taps(n, chunks=3):
                for _n in range(n):
                    open_ = [c for c in range(chunks) if left[c]]
                    if not open_:
                        return
                    c = max(open_, key=lambda c_: (c_ not in undrained, len(left[c_])))
                    if c in undrained:
                        dve.drain()
                        undrained.clear()
                    undrained.add(c)
                    k = left[c].pop(0)
                    if k == 0:
                        dve.tensor_scalar(cout[:, c, :], pad[:, c, 0:T], col("cconv", c), col("cconvb", c), MUL, ADD)
                    else:
                        dve.scalar_tensor_tensor(out=cout[:, c, :], in0=pad[:, c, k:k + T], scalar=col("cconv", 4 * k + c),
                                                 in1=cout[:, c, :], op0=MUL, op1=ADD)

            for c in range(4):
                p = P_AG + 2 * c
                panel_ready(p)
                dve.wait_ge(sg_ready, c + 1)
                dve.scalar_tensor_tensor(out=pad[:, c, TAPS_CONV - 1:], in0=bank[p % RING][:, :], scalar=col("bga", c),
                                         in1=sg[:, c % 2, :], op0=ADD, op1=MUL)
                dve.drain()
                dve.sem_inc(bank_free, 2)
                if c < 3:
                    conv_taps(11, c + 1)
            dve.tensor_scalar(cout[:, 3, :], pad[:, 3, 0:T], col("cconv", 3), col("cconvb", 3), MUL, ADD)\
                .then_inc(pad_ready, 1)

            for c in range(4):
                panel_ready(P_U + c)
                dve.tensor_scalar(u2[:, c, :], bank[(P_U + c) % RING][:, :], col("bu", c), None, ADD).then_inc(bank_free, 1)
                conv_taps(6)
            for p in range(P_V2, P_OUT2, 2):
                at = P * (p - P_V2)
                panel_ready(p + 1)
                for half in range(2):
                    dve.tensor_tensor(v2t[:, 2 * half:2 * half + 2, at:at + 2 * P], tokens_of(p, half),
                                      rows[:, 0:1, at:at + 2 * P].broadcast_to((P, 2, 2 * P)), ADD).then_inc(bank_free, 1)
                conv_taps(10)
            dve.wait_ge(v_gelu, 1)
            for j in range(QB):
                dve.bn_stats(lnst[:, j, 0:6], v2t[:, j, :])
            dve.drain()
            for j in range(QB):
                dve.bn_aggr(lnst[:, j, 6:8], lnst[:, j, 0:6])
            dve.drain()
            dve.sem_inc(var_ready, 1)
            dve.wait_ge(vstd_ready, 1)
            dve.reciprocal(lnst[:, :, 9:10], lnst[:, :, 8:9])
            dve.drain()
            for j in range(QB):
                dve.tensor_scalar(v2t[:, j, :], v2t[:, j, :], lnst[:, j, 6:7], lnst[:, j, 9:10], SUB, MUL)
            dve.drain()
            for j in range(QB):
                dve.tensor_tensor(v2t[:, j, :], v2t[:, j, :], rows[:, 1, :], MUL)
            dve.drain()
            for j in range(QB):
                dve.tensor_tensor(v2t[:, j, :], v2t[:, j, :], rows[:, 2, :], ADD)
            dve.drain()
            dve.sem_inc(vln_ready, 1)
            dve.wait_ge(u_ready, 4)
            for c in range(4):
                dve.wait_ge(mix_done, c + 1)
                dve.drain()
                dve.tensor_tensor(ysp[:, c % 2, :].rearrange("p (j t) -> p j t", j=QB),
                                  bank[4 + c % 2][:, :].rearrange("p (j t) -> p j t", j=QB),
                                  bs[:, c:c + 1, :].broadcast_to((P, QB, P)), ADD).then_inc(bias_added, 1)
                dve.drain()
                dve.tensor_tensor(ysp[:, c % 2, :], ysp[:, c % 2, :], u2[:, c, :], MUL).then_inc(y_ready, 1)
                conv_taps(4)
                dve.wait_ge(y_hi, LC + c + 1)
                dve.drain()
                dve.tensor_tensor(h_lo[:, c, :], ysp[:, c % 2, :], h_hi[:, c, :].bitcast(F32), SUB).then_inc(y_lo, 1)
            conv_taps(3 * TAPS_CONV)
            dve.wait_ge(tap_added, DVE_TAPS3 - 1)
            conv_taps(TAPS_CONV, 4)
            dve.drain()
            dve.tensor_tensor(acc[:, :], cout[:, 0, :], cout[:, 1, :], ADD)
            for c in (2, 3):
                dve.drain()
                m = dve.tensor_tensor(acc[:, :], acc[:, :], cout[:, c, :], ADD)
            m.then_inc(mean_acc, 1)
            dve.wait_ge(mean_done, 1)
            for c in range(4):
                dve.scalar_tensor_tensor(out=cout[:, c, :], in0=bank[6][:, :], scalar=-1.0 / 512, in1=cout[:, c, :],
                                         op0=MUL, op1=ADD).then_inc(centred, 1)
            for c in range(4):
                add_square(6, c)
            rstd(6)

            def conv_low(c):
                dve.wait_ge(y_hi, LC + 4 + c + 1)
                dve.tensor_tensor(h_lo[:, 4 + c, :], ysp[:, c % 2, :], h_hi[:, 4 + c, :].bitcast(F32), SUB)\
                    .then_inc(y_lo, 1)

            for c in range(4):
                dve.drain()
                dve.scalar_tensor_tensor(out=ysp[:, c % 2, :], in0=cout[:, c, :], scalar=col("clng", c), in1=bank[5][:, :],
                                         op0=MUL, op1=MUL).then_inc(cn_ready, 1)
                if c:
                    conv_low(c - 1)
            conv_low(3)
            project(2, P_OUT2, 7)
            norm_h(7)
            ffn(2, P_FFN2, 7)
            norm_h(8)

            dve.wait_ge(rope_landed, 16)
            dve.wait_ge(masks_landed, 48)

            def rotate(n):
                out = q3[:, n, :] if n < KB else k3[:, n - KB, :]
                dve.wait_ge(swap_done, n + 1)
                dve.drain()
                dve.tensor_tensor(rot2[:, :], bank[4 + n % 2][:, :], rope[:, 1, :], MUL).then_inc(rot_done, 1)
                dve.drain()
                dve.tensor_tensor(out, out, rot2[:, :], ADD)

            for p in range(P_Q3, P_V3):
                n = p - P_Q3
                out = q3[:, n, :] if n < KB else k3[:, n - KB, :]
                dve.wait_ge(rot_copied, n + 1)
                dve.tensor_tensor(out, bank[p % RING][:, :], rope[:, 0, :], MUL).then_inc(bank_free, 1)
                if n:
                    rotate(n - 1)
            copy_tokens(P_V3, v3t, 0)
            rotate(2 * KB - 1)
            dve.drain()
            dve.sem_inc(rot_done, 1)
            for p in range(P_V3 + 2, P_OUT3, 2):
                copy_tokens(p, v3t, P * (p - P_V3))
            attention(2)
            project(3, P_OUT3, 9)
            norm_h(9)
            ffn(3, P_FFN3, 9)
            rstd(10)
            for k in range(KB):
                dve.scalar_tensor_tensor(out=yout[:, k, :], in0=x[:, k, :], scalar=gain(10, k), in1=bank[5][:, :],
                                         op0=MUL, op1=MUL).then_inc(yout_ready, 1)


def panel_arrays(w):
    kb, nb = w.shape[0] // P, w.shape[1] // P
    out = np.zeros((nb, P, KB, P), np.float32)
    out[:, :, 0:kb] = w.reshape(kb, P, nb, P).transpose(2, 1, 0, 3)
    return out.reshape(nb, P, KB * P)


def pairs(w, n_pairs):
    return np.ascontiguousarray(w.reshape(w.shape[0], 2, n_pairs, HD).transpose(0, 2, 1, 3).reshape(w.shape[0], -1))


def ffn_panels(wg, wu, wd):
    g, u, out, at = panel_arrays(wg), panel_arrays(wu), [], 0
    for size in PARTS:
        both = np.stack([g[at:at + size], u[at:at + size]], axis=1).reshape(2 * size, P, KB * P)
        out += [both, panel_arrays(wd[P * at:P * (at + size)])]
        at += size
    return out


def laid_out(a):
    f = {k: np.asarray(v) for k, v in a.items()}
    w = f["l0_w_in"]
    n = {"gate": 0, "ax": 512, "q": 1024, "kc": 1536, "vc": 1664, "ks": 1792, "vs": 1920, "kw": 2048, "vw": 2176, "g": 2304}
    parts = [panel_arrays(w[:, 512:1024]), panel_arrays(w[:, 0:512]), panel_arrays(pairs(w[:, 1024:1536], 4))]
    parts += [panel_arrays(w[:, n[k]:n[k] + P]) for k in ("kc", "vc", "ks", "kw", "vs", "vw")]
    parts += [panel_arrays(f["l0_w_out"])]
    parts += ffn_panels(f["l0_ffn_wg"], f["l0_ffn_wu"], f["l0_ffn_wd"])
    w = f["l1_w_in"]
    ki = w[:, 1792:1856]
    index_weights = np.zeros((D, P), np.float32)
    index_weights[:, 0:IDX_HEADS] = w[:, 1856:1864]
    parts += [panel_arrays(w[:, 1280:1792]), panel_arrays(w[:, 1152:1280]), panel_arrays(index_weights),
              panel_arrays(np.concatenate([ki, ki], axis=1)),
              panel_arrays(pairs(w[:, 0:1024], KB)), panel_arrays(w[:, 1024:1152]), panel_arrays(f["l1_w_out"])]
    parts += ffn_panels(f["l1_ffn_wg"], f["l1_ffn_wu"], f["l1_ffn_wd"])
    w = f["even_w_in_2"][0]
    za = panel_arrays(w)
    parts += [np.stack([za[8:12], za[12:16]], axis=1).reshape(8, P, KB * P), za[0:4], za[4:8],
              panel_arrays(f["even_w_out_2"][0])]
    up, down = f["ffn_w_up_2"], f["ffn_w_down_2"]
    parts += ffn_panels(up[0][:, 0:FF], up[0][:, FF:], down[0])
    parts += [panel_arrays(f["odd_w_qkv_2"][0]), panel_arrays(f["odd_w_o_2"][0])]
    parts += ffn_panels(up[1][:, 0:FF], up[1][:, FF:], down[1])
    out = {"panels": np.concatenate(parts)}
    assert out["panels"].shape[0] == N_PANELS
    out["mods"] = np.concatenate([panel_arrays(f["l0_mod_w"]), panel_arrays(f["l1_mod_w"])])

    def c(v_):
        v_ = v_.reshape(-1, P)
        return v_.T

    b_in = f["even_b_in_2"][0]
    named = {
        "c": c(f["c"]), "g0mix": c(f["l0_norm_mix"]), "g0ffn": c(f["l0_norm_ffn"]), "g1mix": c(f["l1_norm_mix"]),
        "g1ffn": c(f["l1_norm_ffn"]), "modb": np.concatenate([c(f["l0_mod_b"]), c(f["l1_mod_b"])], axis=1),
        "lconv": c(f["l0_conv_w"]), "lconvb": c(f["l0_conv_b"]), "ba": c(f["l0_lru_ba"]), "bx": c(f["l0_lru_bx"]),
        "lam": c(f["l0_lru_lambda"]), "final1": c(f["final_norm"]), "even": c(f["even_norm_g_2"]), "bu": c(b_in[0:512]),
        "bga": c(b_in[1024:1536]), "bgg": c(b_in[1536:2048]), "cconv": c(f["even_conv_w_2"][0]),
        "cconvb": c(f["even_conv_b_2"]), "clng": c(f["even_conv_ln_g_2"]), "clnb": c(f["even_conv_ln_b_2"]),
        "odd": c(f["odd_norm_g_2"]), "ffn2": c(f["ffn_norm_g_2"][0]), "ffn3": c(f["ffn_norm_g_2"][1]),
        "fw2": c(f["ffn_conv_w_2"][0]), "fb2": c(f["ffn_conv_b_2"][0]), "fw3": c(f["ffn_conv_w_2"][1]),
        "fb3": c(f["ffn_conv_b_2"][1]), "final2": c(f["final_norm_g_2"]),
    }
    out["cols"] = np.concatenate([named[k] for k in COLS], axis=1)
    assert out["cols"].shape == (P, N_COLS)
    out["x"] = f["x"][0].T.reshape(KB, P, T).transpose(1, 0, 2)

    def per_k(w_):
        return w_.reshape(KB, P, -1).transpose(1, 0, 2)

    out["w_gates"] = per_k(f["l0_w_in"][:, 2304:2328])
    w1 = np.stack([f["l0_cmp_w1_k"], f["l0_cmp_w1_v"]]).reshape(2, CMP_LEN, HD, P).transpose(0, 2, 1, 3)
    out["w1"] = np.concatenate([w1, w1], axis=1)
    out["w2"] = np.stack([f["l0_cmp_w2_k"], f["l0_cmp_w2_v"]], axis=1)
    pe_ = np.stack([f["l0_cmp_pe_k"].T, f["l0_cmp_pe_v"].T], axis=1)
    out["pe"] = np.concatenate([pe_, pe_])
    lru = np.zeros((2, HD, 2, LC, 2, HD), np.float32)
    for b in range(2):
        for w_, name in enumerate(("l0_lru_wa", "l0_lru_wx")):
            lru[b, :, w_, :, b, :] = f[name].reshape(LC, 2, HD, HD)[:, b].transpose(1, 0, 2)
    out["lruw"] = lru.reshape(P, 2, LC, P)
    out["wsT"] = f["even_w_s_2"][0].transpose(2, 0, 1)
    rows = np.stack([b_in[512:1024], f["even_v_ln_g_2"][0], f["even_v_ln_b_2"][0]])
    out["rows"] = np.broadcast_to(rows, (P, 3, 512))
    bs = f["even_b_s_2"][0].reshape(4, 2, 1, P)
    out["bs"] = np.broadcast_to(bs, (4, 2, HD, P)).transpose(1, 2, 0, 3).reshape(P, 4, P)

    t, k = np.arange(T)[:, None], np.arange(T)[None, :]
    by_block = lambda m: m.astype(np.float32).reshape(QB, P, -1).transpose(1, 0, 2)
    out["causal"] = by_block(np.where(k <= t, 0.0, NEG))
    seen = ((t - k >= 0) & (t - k <= 128)).astype(int)
    for dilation in (4, 16):
        seen = seen + ((t >= k) & ((t - k) % dilation == 0))
    out["dilated"] = by_block(np.where(seen > 0, np.log(np.maximum(seen, 1)) / SCALE, NEG))
    ends = np.arange(NCMP) * CMP_STRIDE + CMP_LEN - 1
    cm = np.full((T, 32), NEG)
    cm[:, 0:NCMP] = np.where(ends[None, :] <= t, 0.0, NEG)
    out["cmask"] = by_block(cm)
    half = HD // 2
    inv = np.float32(10000.0) ** (-np.arange(half, dtype=np.float32) / np.float32(half))
    angle = np.arange(T, dtype=np.float32)[None, :] * inv[:, None]
    cos, sin = np.cos(angle), np.sin(angle)
    out["rope"] = np.stack([np.concatenate([cos] * 4), np.concatenate([-sin, sin] * 2)], axis=1).astype(np.float32)
    out["ident"] = np.eye(P, dtype=np.float32)
    out["swap"] = np.eye(P, dtype=np.float32)[np.arange(P) ^ half]
    return {k_: np.ascontiguousarray(v_) for k_, v_ in out.items()}


def kernel(**inputs):
    import concourse.bacc as bacc
    from concourse.bass_utils import run_bass_kernel_spmd

    arrays = laid_out(inputs)
    nc = bacc.Bacc("TRN2", target_bir_lowering=False, num_devices=1)
    A = {k: nc.dram_tensor(f"in_{k}", list(v.shape), mybir.dt.from_np(v.dtype), kind="ExternalInput").ap()
         for k, v in arrays.items()}
    A["out"] = nc.dram_tensor("out_0", [KB, P, T], F32, kind="ExternalOutput").ap()
    build(nc, A)
    r = run_bass_kernel_spmd(nc, [{f"in_{k}": v for k, v in arrays.items()}], core_ids=[0])
    out = r.results[0]["out_0"]
    return np.ascontiguousarray(out.reshape(D, T).T.reshape(1, T, D))
```
